# Optimizing a Trainium2 kernel written in Bass

```python
import math
import jax, jax.numpy as jnp
from jax import lax
import numpy as np

D_MODEL = 1024
BATCH = 1
SEQ = 512
DEPTH = 2

GRID_W = 64
CTX_LEN = 256
ROPE_THETA = 10000.0
EPS = 1e-6
NEG_INF = -1e30
Q_BLOCK = 128
D_FF = 4 * D_MODEL

MLA_HEADS = 8
MLA_NOPE = 64
MLA_ROPE = 32
MLA_V = 64
MLA_Q_RANK = 256
MLA_KV_RANK = 128
MLA_SCALE = (MLA_NOPE + MLA_ROPE) ** -0.5
DIFF_HEADS = 4
DIFF_HD = 64
DIFF_SCALE = DIFF_HD ** -0.5
GQA_HEADS = 8
GQA_KV_HEADS = 2
GQA_GROUP = GQA_HEADS // GQA_KV_HEADS
GQA_HD = 64
NA_HEADS = 8
NA_HD = 64
NA_WIN_ROWS = 8
NA_WIN_COLS = 16
NA_COL_CHUNK = 16
NA_COL_BAND = NA_COL_CHUNK + NA_WIN_COLS
HEAD_SCALE = GQA_HD ** -0.5

EVEN_SPLITS = (MLA_Q_RANK, MLA_KV_RANK, MLA_ROPE,
               DIFF_HEADS * 2 * DIFF_HD, DIFF_HEADS * 2 * DIFF_HD, DIFF_HEADS * 2 * DIFF_HD)
EVEN_IN = sum(EVEN_SPLITS)
EVEN_MIX = MLA_HEADS * MLA_V + DIFF_HEADS * 2 * DIFF_HD
ODD_SPLITS = (GQA_HEADS * GQA_HD, GQA_KV_HEADS * GQA_HD, GQA_KV_HEADS * GQA_HD,
              NA_HEADS * NA_HD, NA_HEADS * NA_HD, NA_HEADS * NA_HD)
ODD_IN = sum(ODD_SPLITS)
ODD_MIX = GQA_HEADS * GQA_HD + NA_HEADS * NA_HD

kernel_name = 'hybrid_flow_backbone'

def rms_norm(x, g):
    xf = x.astype(jnp.float32)
    y = xf * lax.rsqrt(jnp.mean(xf * xf, axis=-1, keepdims=True) + EPS)
    return (y * g.astype(jnp.float32)).astype(x.dtype)

def modulate(u, shift, scale):
    return u * (1 + scale) + shift

def split_cols(p, sizes):
    return jnp.split(p, np.cumsum(sizes)[:-1].tolist(), axis=-1)

def axial_angles(seq_len, rot_dim):
    t = jnp.arange(seq_len, dtype=jnp.int32)
    row = (t // GRID_W).astype(jnp.float32)
    col = (t % GRID_W).astype(jnp.float32)
    n = rot_dim // 4
    inv = ROPE_THETA ** (-jnp.arange(n, dtype=jnp.float32) / n)
    return jnp.concatenate([row[:, None] * inv, col[:, None] * inv], axis=-1)

def apply_rope(x, ang):
    half = x.shape[-1] // 2
    shape = (1, ang.shape[0]) + (1,) * (x.ndim - 3) + (half,)
    cos = jnp.cos(ang).reshape(shape).astype(x.dtype)
    sin = jnp.sin(ang).reshape(shape).astype(x.dtype)
    x1, x2 = x[..., :half], x[..., half:]
    return jnp.concatenate([x1 * cos - x2 * sin, x2 * cos + x1 * sin], axis=-1)

def sweep_query_blocks(fn, *qs):
    b, s = qs[0].shape[:2]
    nb = s // Q_BLOCK
    blocks = tuple(jnp.moveaxis(q.reshape((b, nb, Q_BLOCK) + q.shape[2:]), 1, 0) for q in qs)
    out = lax.map(lambda a: fn(*a), blocks)
    out = jnp.moveaxis(out, 0, 1)
    return out.reshape((b, s) + out.shape[3:])

def attend_mla(q_nope, q_rope, k_nope, k_rope, v):
    s = (jnp.einsum('bqhd,bkhd->bhqk', q_nope, k_nope)
         + jnp.einsum('bqhr,bkr->bhqk', q_rope, k_rope)).astype(jnp.float32) * MLA_SCALE
    p = jax.nn.softmax(s, axis=-1).astype(v.dtype)
    return jnp.einsum('bhqk,bkhd->bqhd', p, v)

def attend_diff(q, k, v, lam):
    s = jnp.einsum('bqhmd,bkhmd->bhmqk', q, k).astype(jnp.float32) * DIFF_SCALE
    p = jax.nn.softmax(s, axis=-1)
    p = p[:, :, 0] - lam * p[:, :, 1]
    return jnp.einsum('bhqk,bkhv->bqhv', p.astype(v.dtype), v)

def attend_gqa(q, k, v):
    s = jnp.einsum('bqhgd,bkhd->bhgqk', q, k).astype(jnp.float32) * HEAD_SCALE
    p = jax.nn.softmax(s, axis=-1).astype(v.dtype)
    return jnp.einsum('bhgqk,bkhd->bqhgd', p, v)

def neighbourhood_attention(q, k, v, k_ctx, v_ctx, rpb):
    b, s, h, d = q.shape
    rows = s // GRID_W
    win_r = min(NA_WIN_ROWS, rows)
    n_chunks = GRID_W // NA_COL_CHUNK
    q_col = np.arange(GRID_W).reshape(n_chunks, NA_COL_CHUNK)
    band_start = np.clip(q_col[:, 0] - NA_WIN_COLS // 2, 0, GRID_W - NA_COL_BAND)
    key_col = band_start[:, None] + np.arange(NA_COL_BAND)
    win_start = np.clip(q_col - NA_WIN_COLS // 2, 0, GRID_W - NA_WIN_COLS)
    col_mask = ((key_col[:, None, :] >= win_start[..., None])
                & (key_col[:, None, :] < win_start[..., None] + NA_WIN_COLS))
    rel_col_idx = np.clip(key_col[:, None, :] - q_col[..., None] + NA_WIN_COLS - 1,
                          0, 2 * NA_WIN_COLS - 2)
    kg = k.reshape(b, rows, GRID_W, h, d)
    vg = v.reshape(b, rows, GRID_W, h, d)
    qg = q.reshape(b, rows, n_chunks, NA_COL_CHUNK, h, d)
    n_ctx = k_ctx.shape[1]

    def row_block(args):
        r, q_row = args
        r0 = jnp.clip(r - win_r // 2, 0, rows - win_r)
        k_band = lax.dynamic_slice_in_dim(kg, r0, win_r, axis=1)
        v_band = lax.dynamic_slice_in_dim(vg, r0, win_r, axis=1)
        k_sub = k_band[:, :, key_col]
        v_sub = v_band[:, :, key_col]
        s_loc = jnp.einsum('bjqhd,bijkhd->bhjqik', q_row, k_sub).astype(jnp.float32) * HEAD_SCALE
        rel_row = r0 + jnp.arange(win_r) - r + NA_WIN_ROWS - 1
        bias = rpb[:, rel_row[None, None, :, None], rel_col_idx[:, :, None, :]]
        s_loc = jnp.where(col_mask[:, :, None, :], s_loc + bias[None].astype(jnp.float32), NEG_INF)
        s_loc = s_loc.reshape(b, h, n_chunks, NA_COL_CHUNK, win_r * NA_COL_BAND)
        s_ctx = jnp.einsum('bjqhd,bkhd->bhjqk', q_row, k_ctx).astype(jnp.float32) * HEAD_SCALE
        p = jax.nn.softmax(jnp.concatenate([s_ctx, s_loc], axis=-1), axis=-1).astype(v.dtype)
        p_ctx = p[..., :n_ctx]
        p_loc = p[..., n_ctx:].reshape(b, h, n_chunks, NA_COL_CHUNK, win_r, NA_COL_BAND)
        return (jnp.einsum('bhjqk,bkhd->bjqhd', p_ctx, v_ctx)
                + jnp.einsum('bhjqik,bijkhd->bjqhd', p_loc, v_sub))

    out = lax.map(row_block, (jnp.arange(rows), jnp.moveaxis(qg, 1, 0)))
    return jnp.moveaxis(out, 0, 1).reshape(b, s, h, d)

def even_mixer(a_lat, a_ctx, w_in, w_out, mla_q_norm, mla_w_uq, mla_kv_norm, mla_w_ukv,
               diff_lambda, diff_subln, lam_init, ang_mla, ang_head, want_ctx):
    lp = diff_lambda.astype(jnp.float32)
    lam = jnp.exp(jnp.sum(lp[0] * lp[1])) - jnp.exp(jnp.sum(lp[2] * lp[3])) + lam_init

    def project(a, rope):
        b, t, _ = a.shape
        cq, ckv, kr, dq, dk, dv = split_cols(a @ w_in, EVEN_SPLITS)
        q = (rms_norm(cq, mla_q_norm) @ mla_w_uq).reshape(b, t, MLA_HEADS, MLA_NOPE + MLA_ROPE)
        kv = (rms_norm(ckv, mla_kv_norm) @ mla_w_ukv).reshape(b, t, MLA_HEADS, MLA_NOPE + MLA_V)
        qn, qr = q[..., :MLA_NOPE], q[..., MLA_NOPE:]
        kn, v = kv[..., :MLA_NOPE], kv[..., MLA_NOPE:]
        dq = dq.reshape(b, t, DIFF_HEADS, 2, DIFF_HD)
        dk = dk.reshape(b, t, DIFF_HEADS, 2, DIFF_HD)
        dv = dv.reshape(b, t, DIFF_HEADS, 2 * DIFF_HD)
        if rope:
            qr, kr = apply_rope(qr, ang_mla), apply_rope(kr, ang_mla)
            dq, dk = apply_rope(dq, ang_head), apply_rope(dk, ang_head)
        return qn, qr, kn, kr, v, dq, dk, dv

    def merge(o_mla, o_diff):
        b, t = o_mla.shape[:2]
        o_diff = rms_norm(o_diff, diff_subln) * (1.0 - lam_init)
        return jnp.concatenate([o_mla.reshape(b, t, -1), o_diff.reshape(b, t, -1)], axis=-1) @ w_out

    qn_c, qr_c, kn_c, kr_c, v_c, dq_c, dk_c, dv_c = project(a_ctx, False)
    qn, qr, kn, kr, v, dq, dk, dv = project(a_lat, True)
    cat = lambda u, w: jnp.concatenate([u, w], axis=1)
    kn_all, kr_all, v_all = cat(kn_c, kn), cat(kr_c, kr), cat(v_c, v)
    dk_all, dv_all = cat(dk_c, dk), cat(dv_c, dv)
    o_lat = merge(sweep_query_blocks(lambda a, b: attend_mla(a, b, kn_all, kr_all, v_all), qn, qr),
                  sweep_query_blocks(lambda a: attend_diff(a, dk_all, dv_all, lam), dq))
    o_ctx = None
    if want_ctx:
        o_ctx = merge(attend_mla(qn_c, qr_c, kn_c, kr_c, v_c), attend_diff(dq_c, dk_c, dv_c, lam))
    return o_lat, o_ctx

def odd_mixer(a_lat, a_ctx, w_in, w_out, gqa_qk_norm, na_rpb, ang_head, want_ctx):
    def project(a, rope):
        b, t, _ = a.shape
        gq, gk, gv, nq, nk, nv = split_cols(a @ w_in, ODD_SPLITS)
        gq = rms_norm(gq.reshape(b, t, GQA_KV_HEADS, GQA_GROUP, GQA_HD), gqa_qk_norm[0])
        gk = rms_norm(gk.reshape(b, t, GQA_KV_HEADS, GQA_HD), gqa_qk_norm[1])
        gv = gv.reshape(b, t, GQA_KV_HEADS, GQA_HD)
        nq = nq.reshape(b, t, NA_HEADS, NA_HD)
        nk = nk.reshape(b, t, NA_HEADS, NA_HD)
        nv = nv.reshape(b, t, NA_HEADS, NA_HD)
        if rope:
            gq, gk = apply_rope(gq, ang_head), apply_rope(gk, ang_head)
        return gq, gk, gv, nq, nk, nv

    def merge(o_gqa, o_na):
        b, t = o_gqa.shape[:2]
        return jnp.concatenate([o_gqa.reshape(b, t, -1), o_na.reshape(b, t, -1)], axis=-1) @ w_out

    gq_c, gk_c, gv_c, nq_c, nk_c, nv_c = project(a_ctx, False)
    gq, gk, gv, nq, nk, nv = project(a_lat, True)
    gk_all = jnp.concatenate([gk_c, gk], axis=1)
    gv_all = jnp.concatenate([gv_c, gv], axis=1)
    o_lat = merge(sweep_query_blocks(lambda a: attend_gqa(a, gk_all, gv_all), gq),
                  neighbourhood_attention(nq, nk, nv, nk_c, nv_c, na_rpb))
    o_ctx = None
    if want_ctx:
        o_ctx = merge(attend_gqa(gq_c, gk_c, gv_c), attend_gqa(nq_c[:, :, :, None], nk_c, nv_c))
    return o_lat, o_ctx

def channel_mixer(a, w1, w2):
    return jnp.square(jax.nn.relu(a @ w1)) @ w2

def setup_inputs(seed: int = 0) -> dict:
    key = jax.random.key(seed)
    ks = jax.random.split(key, 22)
    n_even, n_odd = (DEPTH + 1) // 2, DEPTH // 2
    f32 = jnp.float32
    nrm = lambda k, shape: jax.random.normal(k, shape, f32)
    lin = lambda k, shape, fan_in: nrm(k, shape) * fan_in ** -0.5
    gain = lambda k, shape: 1.0 + 0.02 * nrm(k, shape)
    return {
        'x': nrm(ks[0], (BATCH, SEQ, D_MODEL)),
        'c': nrm(ks[1], (BATCH, D_MODEL)),
        'ctx': nrm(ks[2], (BATCH, CTX_LEN, D_MODEL)),
        'c_ctx': nrm(ks[3], (D_MODEL,)),
        'w_ada': lin(ks[4], (DEPTH, D_MODEL, 6 * D_MODEL), D_MODEL),
        'b_ada': 0.01 * nrm(ks[5], (DEPTH, 6 * D_MODEL)),
        'norm_g': gain(ks[6], (DEPTH, 4, D_MODEL)),
        'w_ff1': lin(ks[7], (DEPTH, D_MODEL, D_FF), D_MODEL),
        'w_ff2': lin(ks[8], (DEPTH, D_FF, D_MODEL), D_FF),
        'w_in_even': lin(ks[9], (n_even, D_MODEL, EVEN_IN), D_MODEL),
        'w_out_even': lin(ks[10], (n_even, EVEN_MIX, D_MODEL), EVEN_MIX),
        'mla_q_norm': gain(ks[11], (n_even, MLA_Q_RANK)),
        'mla_w_uq': lin(ks[12], (n_even, MLA_Q_RANK, MLA_HEADS * (MLA_NOPE + MLA_ROPE)), MLA_Q_RANK),
        'mla_kv_norm': gain(ks[13], (n_even, MLA_KV_RANK)),
        'mla_w_ukv': lin(ks[14], (n_even, MLA_KV_RANK, MLA_HEADS * (MLA_NOPE + MLA_V)), MLA_KV_RANK),
        'diff_lambda': 0.1 * nrm(ks[15], (n_even, 4, DIFF_HD)),
        'diff_subln': gain(ks[16], (n_even, 2 * DIFF_HD)),
        'w_in_odd': lin(ks[17], (n_odd, D_MODEL, ODD_IN), D_MODEL),
        'w_out_odd': lin(ks[18], (n_odd, ODD_MIX, D_MODEL), ODD_MIX),
        'gqa_qk_norm': gain(ks[19], (n_odd, 2, GQA_HD)),
        'na_rpb': 0.1 * nrm(ks[20], (n_odd, NA_HEADS, 2 * NA_WIN_ROWS - 1, 2 * NA_WIN_COLS - 1)),
    }

def reference(x, c, ctx, c_ctx, w_ada, b_ada, norm_g, w_ff1, w_ff2,
              w_in_even, w_out_even, mla_q_norm, mla_w_uq, mla_kv_norm, mla_w_ukv,
              diff_lambda, diff_subln, w_in_odd, w_out_odd, gqa_qk_norm, na_rpb):
    seq = x.shape[1]
    ang_mla = axial_angles(seq, MLA_ROPE)
    ang_head = axial_angles(seq, GQA_HD)
    silu_c, silu_cc = jax.nn.silu(c), jax.nn.silu(c_ctx)
    h, hc = x, ctx
    for layer in range(DEPTH):
        want_ctx = layer < DEPTH - 1
        mod = jnp.split((silu_c @ w_ada[layer] + b_ada[layer])[:, None, :], 6, axis=-1)
        mod_c = jnp.split(silu_cc @ w_ada[layer] + b_ada[layer], 6, axis=-1)
        g = norm_g[layer]
        a_lat = modulate(rms_norm(h, g[0]), mod[0], mod[1])
        a_ctx = modulate(rms_norm(hc, g[0]), mod_c[0], mod_c[1])
        i = layer // 2
        if layer % 2 == 0:
            lam_init = 0.8 - 0.6 * math.exp(-0.3 * layer)
            o_lat, o_ctx = even_mixer(a_lat, a_ctx, w_in_even[i], w_out_even[i], mla_q_norm[i], mla_w_uq[i],
                                      mla_kv_norm[i], mla_w_ukv[i], diff_lambda[i], diff_subln[i],
                                      lam_init, ang_mla, ang_head, want_ctx)
        else:
            o_lat, o_ctx = odd_mixer(a_lat, a_ctx, w_in_odd[i], w_out_odd[i], gqa_qk_norm[i], na_rpb[i],
                                     ang_head, want_ctx)
        h = h + mod[2] * rms_norm(o_lat, g[1])
        f = channel_mixer(modulate(rms_norm(h, g[2]), mod[3], mod[4]), w_ff1[layer], w_ff2[layer])
        h = h + mod[5] * rms_norm(f, g[3])
        if want_ctx:
            hc = hc + mod_c[2] * rms_norm(o_ctx, g[1])
            fc = channel_mixer(modulate(rms_norm(hc, g[2]), mod_c[3], mod_c[4]), w_ff1[layer], w_ff2[layer])
            hc = hc + mod_c[5] * rms_norm(fc, g[3])
    return h


_drawn_inputs = setup_inputs


def setup_inputs(seed=0):
    import zlib

    import numpy as np

    out = dict(_drawn_inputs(seed))
    spreads = {}
    factors = {'b_ada': 2.724,
     'mla_q_norm': 8.0,
     'mla_kv_norm': 8.0,
     'diff_subln': 18.868,
     'gqa_qk_norm': 8.0,
     'na_rpb': 8.0}
    for name, (base, spread) in spreads.items():
        noise = np.random.default_rng([zlib.crc32(name.encode()), seed]).standard_normal(out[name].shape)
        drawn = base * np.exp(spread * noise) if base else spread * noise
        out[name] = __import__('jax').numpy.asarray(drawn.astype(out[name].dtype))
    for name, factor in factors.items():
        out[name] = (out[name] * factor).astype(out[name].dtype)
    return out
```

```python
from contextlib import ExitStack

import numpy as np

import concourse.bass as bass
from concourse import mybir

F32 = mybir.dt.float32
F32R = mybir.dt.float32r
BF16 = mybir.dt.bfloat16
I32 = mybir.dt.int32
ALU = mybir.AluOpType
ACT = mybir.ActivationFunctionType
AX = mybir.AxisListType

P = 128
D = 1024
KT = D // P
SEQ, CTX = 512, 256
TOK = SEQ + CTX
NT, NTL = TOK // P, SEQ // P
DFF = 4 * D
GRID_W, ROWS = 64, 8
EPS = 1e-6
UW = 256
UE = KT * UW
MLA_H, NOPE, ROPE, QH = 8, 64, 32, 96
MLA_SCALE = float(QH) ** -0.5
HEAD_SCALE = 0.125
LAM_INIT = 0.8 - 0.6
CHUNKS, CC, BAND = 4, 16, 32
BAND_START = [min(max(CC * j - 8, 0), GRID_W - BAND) for j in range(CHUNKS)]
EVEN_STARTS = [0, 256, 416, 672, 928, 1184, 1440, 1696]
ODD_STARTS = [UW * u for u in range(9)]
ODD_KINDS = ["gq", "gq", "gkv", "nq", "nq", "nk", "nk", "nv", "nv"]
FF_CHUNKS = DFF // (2 * UW)
C_G, C_B, C_C, C_QG, C_KG, C_SUB, C_END = 0, 64, 160, 176, 178, 179, 180
K_ID, K_ONE, K_END = 0, 128, 256
T_CH, T_SH, T_CM, T_SM, T_END = 0, 32, 96, 112, 144


def attention_steps(layer):
    if layer == 0:
        return ([("mla", h, t) for h in range(MLA_H) for t in range(NT)]
                + [("diff", h, t) for h in range(4) for t in range(NT)])
    return ([("gqa", h, t) for h in range(8) for t in range(NTL)]
            + [("na", h, j) for j in range(CHUNKS) for h in range(8)])


def side_jobs():
    jobs, unit = [], 8
    for kind, h, t in attention_steps(0):
        here = []
        if kind == "mla" and h + 1 < MLA_H and t < 4:
            here.append(("head", h + 1, t))
        elif unit < 48:
            here.append(("ada", unit, 0))
            unit += 1
        jobs.append(here)
    jobs[-1].append(("flush", 47, 0))
    assert unit == 48
    return jobs


def build(nc, x, ctx, cols, rows, consts, tables, na_bias, w_ada, w_ff1, w_ff2, w_in_even,
          w_out_even, w_uq, w_ukv, w_in_odd, w_out_odd, out):
    steps = [attention_steps(0), attention_steps(1)]
    jobs = side_jobs()

    def win(w, c0):
        return w.rearrange("(k p) n -> p k n", p=P)[:, :, c0:c0 + UW]

    loads = [("s", win(w_ada[0], UW * a)) for a in range(8)]
    loads += [("s", win(w_in_even[0], c0)) for c0 in EVEN_STARTS]
    for here in jobs:
        loads += [("s", win(w_ada[a // 24], UW * (a % 24))) for kind, a, _ in here if kind == "ada"]
    loads += [("s", win(w_out_even[0], UW * u)) for u in range(4)]
    loads_ff0 = len(loads)
    loads += [("ff", None)] * 32
    loads += [("s", win(w_in_odd[0], c0)) for c0 in ODD_STARTS]
    loads += [("bias", na_bias[j].rearrange("p h k -> p (h k)")) for j in range(CHUNKS)]
    loads += [("s", win(w_out_odd[0], UW * u)) for u in range(4)]
    loads_ff1 = len(loads)
    loads += [("ff", None)] * 32

    with ExitStack() as stack:
        sem = lambda name: stack.enter_context(nc.semaphore(name))
        at = [1152]

        def place(name, shape, dt, offset=None):
            size = int(np.prod(shape[1:])) * (2 if dt == BF16 else 4)
            if offset is None:
                offset = at[0]
                at[0] += (size + 31) // 32 * 32
            return nc.alloc_sbuf_tensor_at(name, shape, dt, offset=offset)

        KB = 1024
        raw = [place(f"raw{i}", [P, KT, UW], F32) for i in range(2)]
        whi = [place(f"whi{i}", [P, KT, UW], F32R) for i in range(2)]
        wlo = [place(f"wlo{i}", [P, KT, UW], F32R) for i in range(2)]
        H = at[0]
        h = place("h", [P, NT, D], F32)
        dqz = place("dqz", [P, 8, TOK], F32, H)
        A = at[0]
        ahi = place("ahi", [P, KT, TOK], F32R)
        alo = place("alo", [P, KT, TOK], F32R)
        B = at[0]
        xn = place("xn", [P, NT, D], F32)
        C = at[0]
        uhi = place("uhi", [P, KT, TOK], F32R)
        ulo = place("ulo", [P, KT, TOK], F32R)
        first_raw = [place(f"first_raw{i}", [P, KT, UW], F32, A + 8 * KB * i) for i in range(6)]
        otok = place("otok", [P, NT, D], F32, A)
        prob = place("prob", [P, 4, TOK], F32, A + 24 * KB)
        vmla = place("vmla", [P, NT, 512], F32, A + 36 * KB)
        cqT = place("cqT", [P, 2, TOK], F32, B)
        qrT = place("qrT", [P, 2, TOK], F32, B + 6 * KB)
        stage = place("stage", [P, 2, NT, UW], F32, B + 12 * KB)
        qslot = place("qslot", [P, 2, TOK], F32, B + 12 * KB)
        kslot = place("kslot", [P, 2, TOK], F32, B + 18 * KB)
        wuq = place("wuq", [P, 2, MLA_H * QH], F32, C)
        wukv = place("wukv", [P, MLA_H * P], F32, C + 6 * KB)
        dkT = place("dkT", [P, 4, TOK], F32, C + 10 * KB)
        dv = place("dv", [P, NT, 512], F32, C + 22 * KB)
        gkT = place("gkT", [P, 2, TOK], F32, B)
        gv = place("gv", [P, NT, P], F32, B + 6 * KB)
        gqz = place("gqz", [P, 8, SEQ], F32, C)
        nqz = place("nqz", [P, 8, SEQ], F32, C + 16 * KB)
        nkT = place("nkT", [P, 4, TOK], F32, C + 32 * KB)
        nvb = place("nvb", [P, CHUNKS, 2, 512], F32, A + 16 * KB)
        prob1 = place("prob1", [P, 4, TOK], F32, A + 36 * KB)
        G = at[0]
        gate = place("gate", [P, 2, D], F32)
        mods4 = place("mods4", [P, 96, 4], F32, G)
        S2 = at[0]
        relu = place("relu", [P, 2, TOK], F32)
        rsq = place("rsq", [P, 2, TOK], F32)
        tmp = place("tmp", [P, 4, 512], F32, S2)
        pT = place("pT", [P, 2, NT, P], F32, S2)
        sqj = place("sqj", [P, NT, UW], F32, S2)
        ckvT = place("ckvT", [P, TOK], F32, S2 + 6 * KB)
        nvc = place("nvc", [P, 2, 512], F32, S2 + 6 * KB)
        junk = place("junk", [P, D], BF16, S2 + 8 * KB)
        junk2 = place("junk2", [P, UW], BF16, S2 + 9 * KB)
        rt1 = place("rt1", [P, UW], F32, S2 + 10 * KB)
        rt2 = place("rt2", [P, UW], F32, S2 + 11 * KB)
        modrow = [place("modrow0", [4, UW], F32, S2 + 10 * KB), place("modrow1", [4, UW], F32, S2 + 11 * KB)]
        krT = place("krT", [32, TOK], F32)
        diag = place("diag", [P, 4, P], F32, at[0] - 3 * KB)
        kons = place("kons", [P, K_END], F32)
        tabs = place("tabs", [P, NTL, T_END], F32)
        colv = place("colv", [P, C_END], F32)
        rowv = place("rowv", [P, 384], F32)
        mods = place("mods", [P, 96, 2], F32)
        scl = place("scl", [P, 2, 2, KT, 2], F32)
        gcol = place("gcol", [P, 2, 2, KT, 2], F32)
        silu = place("silu", [P, KT, 2], F32)
        silu4 = place("silu4", [P, KT, 4], F32R)
        sexp = place("sexp", [P, 2 * KT], F32)
        subc = place("subc", [P, 1], F32)
        lamt = place("lamt", [P, 2], F32)
        neglam = place("neglam", [P, 1], F32)
        ss = place("ss", [P, 24], F32)
        chv = place("chv", [P, 24], F32)
        chi = place("chi", [P, 24], I32)
        cha = place("cha", [P, 24], F32)
        chy = place("chy", [P, 24], F32)
        rstd = place("rstd", [P, 24], F32)
        token = place("token", [P, 1], F32)
        nmax = place("nmax", [P, 4], F32)
        rsum = place("rsum", [P, 4], F32)
        rinv = place("rinv", [P, 4], F32)
        assert at[0] <= 229344, at[0]
        ident = kons[:, K_ID:K_ID + P]
        ones = kons[:, K_ONE:K_ONE + P]
        ps = stack.enter_context(nc.psum_tensor("ps", [P, 8 * 512], F32))
        bank = lambda b, n=512, rows=P: ps[0:rows, 512 * b:512 * b + n]

        s_raw = [sem("raw_loaded0"), sem("raw_loaded1")]
        s_first = [sem(f"first_raw_loaded{i}") for i in range(6)]
        s_small = sem("small_loaded")
        s_x = sem("x_loaded")
        s_mlaw = sem("mla_weights_loaded")
        s_band = sem("band_values_moved")
        s_out = sem("out_stored")
        s_job = sem("side_job_done")
        s_tg = sem("transposes_done")
        s_g = sem("product_done")
        s_f1 = sem("hidden_done")
        s_f2 = sem("down_done")
        s_s = sem("scores_done")
        s_t = sem("probs_transposed")
        s_pv = sem("values_done")
        s_hi = sem("weights_hi_done")
        s_jobf = sem("side_job_copied")
        s_tga = sem("even_group_copied")
        s_gf = sem("product_copied")
        s_relu = sem("relu_done")
        s_uhi = sem("hidden_hi_done")
        s_thi = sem("activations_hi_done")
        s_sq = sem("squares_summed")
        s_ex = sem("exp_done")
        s_ptb = sem("probs_b_copied")
        s_ac = sem("scalar_chain")
        s_lo = sem("weights_lo_done")
        s_tgd = sem("odd_group_copied")
        s_tlo = sem("activations_lo_done")
        s_xn = sem("normed")
        s_res = sem("residual_added")
        s_rsq = sem("relu_squared")
        s_ulo = sem("hidden_lo_done")
        s_f2f = sem("down_added")
        s_mx = sem("max_done")
        s_pc = sem("diff_probs_combined")
        s_pta = sem("probs_a_copied")
        s_oe = sem("head_output_copied")
        s_dg = sem("gate_diagonal_done")
        s_post = sem("stage_processed")
        s_vc = sem("vector_chain")
        s_qr = sem("rope_rows_copied")
        s_mod = sem("mods_ready")
        s_silu = sem("silu_ready")
        s_zero = sem("accumulator_zeroed")

        tg_index = {}
        tg_list = []

        def group(name):
            tg_index[name] = len(tg_list)
            tg_list.append(name)

        def norm_groups(tag, nt):
            for k in range(KT):
                group((tag, k, 0))
                if nt > NTL:
                    group((tag, k, 1))

        streams = {0: (0, 1), 1: (0,)}
        norm_groups("pre00", NT)
        inproj0 = {u: ([(f, s) for f in range(2) for s in (0, 1)] if u not in (1, 6, 7) else
                       [(0, 0), (0, 1), (1, 0), (1, 1)] if u == 1 else []) for u in range(8)}
        for u in range(8):
            for fs in inproj0[u]:
                group(("in0", u) + fs)
        for fs in [(f, s) for f in range(2) for s in (0, 1)]:
            group(("qr",) + fs)
        norm_groups("out0", NT)
        for s in streams[0]:
            for half in range(2):
                group(("gate00", s, half))
        norm_groups("pre01", NT)
        for s in streams[0]:
            for half in range(2):
                group(("gate01", s, half))
        norm_groups("pre10", NT)
        inproj1 = {}
        for u, kind in enumerate(ODD_KINDS):
            both = (0,) if kind in ("gq", "nq") else (0, 1)
            inproj1[u] = [] if kind == "nv" else [(f, s) for f in range(2) for s in both]
            for fs in inproj1[u]:
                group(("in1", u) + fs)
        norm_groups("out1", NTL)
        for half in range(2):
            group(("gate10", 0, half))
        norm_groups("pre11", NTL)
        for half in range(2):
            group(("gate11", 0, half))

        def wait_group_copied(eng, n):
            if n < 0:
                return
            eng.wait_ge(s_tga if n % 2 == 0 else s_tgd, n // 2 + 1)

        def wait_groups_before(eng, n):
            wait_group_copied(eng, n - 1)
            wait_group_copied(eng, n - 2)

        def span(s):
            return slice(0, SEQ) if s == 0 else slice(SEQ, TOK)

        def tiles(s):
            return range(0, NTL) if s == 0 else range(NTL, NT)

        W_IN0, W_ADA, W_OUT0, W_FF0 = 8, 16, 56, 60
        W_IN1 = W_FF0 + 32
        W_OUT1 = W_IN1 + 9
        W_FF1 = W_OUT1 + 4
        G_IN0 = 0
        G_QR = G_IN0 + 8 * NT
        G_V = G_QR + NT
        G_OUT0 = G_V + NT
        G_IN1 = G_OUT0 + 4 * NT
        in1_tiles = [NTL if k in ("gq", "nq") else NT for k in ODD_KINDS]
        G_OUT1 = G_IN1 + sum(in1_tiles)
        G_END = G_OUT1 + 4 * NTL
        n_steps0 = len(steps[0])
        s_first_, count = {}, 0
        for layer in range(2):
            for i, st in enumerate(steps[layer]):
                s_first_[layer, i] = count
                count += 2 if st[0] == "diff" else 1
        S_TOTAL = count
        T0 = {0: 0, 1: n_steps0}
        raw_index = {"ff0": loads_ff0, "ff1": loads_ff1}
        raw_of_unit = [r for r, l in enumerate(loads) if l[0] in ("s", "ff")]
        ada_unit = lambda a: a if a < 8 else W_ADA + a - 8
        bias_raw = [r for r, l in enumerate(loads) if l[0] == "bias"]
        job_count = 8
        job_index = {("ada", a, 0): a for a in range(8)}
        job_index["flush", 7, 0] = job_count
        job_count += 1
        for t in range(4):
            job_index["head", 0, t] = job_count
            job_count += 1
        for here in jobs:
            for j in here:
                job_index[j] = job_count
                job_count += 1

        SQ = {"pre00": 0, "cq": 6, "ckv": 12, "post00": 18, "pre01": 24, "post01": 30, "pre10": 36,
              "post10": 42, "pre11": 46, "post11": 50}
        XN = {"pre00": 0, "pre01": 6, "pre10": 12, "pre11": 18}
        RES = {"00": 0, "01": 6, "10": 12, "11": 16}
        TS = {"pre00": 0, "out0": 16, "pre01": 32, "pre10": 48, "out1": 64, "pre11": 72, "end": 80}
        NSTREAM = {"pre00": 2, "out0": 2, "pre01": 2, "pre10": 2, "out1": 1, "pre11": 1}
        POST = {"in0": 0, "qr": 6, "diffnorm": 7, "in1": 8}

        dg_index = {}
        for tag, layer in (("gate00", 0), ("gate01", 0), ("gate10", 1), ("gate11", 1)):
            for s in streams[layer]:
                for half in range(2):
                    dg_index[tag, s, half] = len(dg_index)

        def norm_list(tag):
            return [(k, s) for k in range(KT) for s in range(NSTREAM[tag])]

        def step_info(layer, i):
            kind, hd, t = steps[layer][i]
            tcol = slice(P * t, P * t + P)
            keys = [(0, SEQ), (SEQ, TOK)] if (layer == 1 or t < NTL) else [(SEQ, TOK)]
            ktiles = list(range(NT)) if (layer == 1 or t < NTL) else list(range(NTL, NT))
            if kind == "mla":
                sc = [(qslot[0:QH, hd % 2, tcol], [kslot[0:QH, hd % 2, a:b] for a, b in keys])]
                vals = [vmla[:, k, P * (hd // 2):P * (hd // 2) + P] for k in ktiles]
                return sc, vals, otok[:, t, 64 * hd:64 * hd + 64]
            if kind == "diff":
                sc = [(dqz[:, 2 * hd + m, tcol], [dkT[:, hd, a:b] for a, b in keys]) for m in range(2)]
                vals = [dv[:, k, P * hd:P * hd + P] for k in ktiles]
                return sc, vals, otok[:, t, 512 + P * hd:512 + P * hd + P]
            if kind == "gqa":
                sc = [(gqz[:, hd, tcol], [gkT[:, hd // 4, a:b] for a, b in keys])]
                vals = [gv[:, k, :] for k in ktiles]
                return sc, vals, otok[:, t, 64 * hd:64 * hd + 64]
            kk = nkT[:, hd // 2, 0:SEQ].rearrange("p (r c) -> p r c", c=GRID_W)
            b0 = BAND_START[t]
            sc = [(nqz[:, hd, tcol], [kk[:, :, b0:b0 + BAND], nkT[:, hd // 2, SEQ:TOK]])]
            pair = slice(P * (hd // 2), P * (hd // 2) + P)
            vals = [nvb[:, t, k, pair] for k in range(2)] + [nvc[:, k, pair] for k in range(2)]
            return sc, vals, otok[:, t, 512 + 64 * hd:512 + 64 * hd + 64]

        def value_half(layer, i):
            kind, hd, _ = steps[layer][i]
            return 64 * (hd // 4 if kind == "gqa" else hd % 2)

        probs = [prob, prob1]

        block = stack.enter_context(nc.Block())

        @block.sync
        def _(sp):
            sp.dma_start(colv[:, :], cols).then_inc(s_small, 16)
            sp.dma_start(rowv[:, :], rows.partition_broadcast(P)).then_inc(s_small, 16)
            sp.dma_start(kons[:, :], consts).then_inc(s_small, 16)
            sp.dma_start(tabs[:, :, :], tables.rearrange("(t p) n -> p t n", p=P)).then_inc(s_small, 16)
            def load_h():
                sp.dma_start(h[:, 0:NTL, :], x[0].rearrange("(t p) d -> p t d", p=P)).then_inc(s_x, 16)
                sp.dma_start(h[:, NTL:NT, :], ctx[0].rearrange("(t p) d -> p t d", p=P)).then_inc(s_x, 16)

            for r in range(6):
                if r == 3:
                    load_h()
                sp.dma_start(first_raw[r][:, :, :], loads[r][1]).then_inc(s_first[r], 16)
            sp.dma_start(wuq[:, :, :], w_uq[0].rearrange("(k p) n -> p k n", p=P)).then_inc(s_mlaw, 16)
            sp.dma_start(wukv[:, :], w_ukv[0]).then_inc(s_mlaw, 16)

            def slot_free(r):
                if loads[r][0] == "bias":
                    sp.wait_ge(s_mx, s_first_[1, 32 + 8 * bias_raw.index(r) + 7] + 1)
                else:
                    sp.wait_ge(s_lo, raw_of_unit.index(r) + 1)

            def ff_load(layer, kind, chunk, half, r, unit_before):
                if unit_before is not None:
                    sp.wait_ge(s_lo, unit_before + 1)
                if kind == 1:
                    src = w_ff1[layer].rearrange("(k p) n -> p k n", p=P)[
                        :, :, bass.ds(chunk * 512 + UW * half, UW)]
                    dst = raw[r % 2][:, :, :]
                else:
                    src = w_ff2[layer].rearrange("(c k p) n -> c p k n", p=P, k=4)[
                        bass.ds(chunk, 1), :, :, 512 * half:512 * half + 512].rearrange("c p k n -> p (c k) n")
                    dst = raw[r % 2][:, :, :].rearrange("p k n -> p (k n)").rearrange("p (k n) -> p k n", n=512)
                sp.dma_start(dst, src).then_inc(s_raw[r % 2], 16)

            def band_moves():
                sp.wait_ge(s_gf, G_OUT1)
                for u in (7, 8):
                    for j in range(CHUNKS):
                        for i in range(4):
                            src_p = GRID_W * (i % 2) + BAND_START[j]
                            src = stage[src_p:src_p + BAND, u % 2, i // 2:i // 2 + 3:2, :]
                            dst = nvb[BAND * i:BAND * i + BAND, j, :, UW * (u - 7):UW * (u - 7) + UW]
                            sp.dma_start(dst, src).then_inc(s_band, 16)

            def straight(r0, r1):
                for r in range(r0, r1):
                    kind, src = loads[r]
                    if kind == "bias" and r == bias_raw[0]:
                        band_moves()
                    if r >= 8:
                        slot_free(r - 2)
                    if r == W_OUT0 + 2:
                        sp.wait_ge(s_s, s_first_[1, 0])
                        load_h()
                    dst = raw[r % 2][:, :, :]
                    if kind == "bias":
                        dst = dst.rearrange("p k n -> p (k n)")
                    sp.dma_start(dst, src).then_inc(s_raw[r % 2], 16)

            def ff(layer, r0, w0):
                ff_load(layer, 1, 0, 0, r0, w0 - 2)
                ff_load(layer, 1, 0, 1, r0 + 1, w0 - 1)

                def pair(c, dyn):
                    u = w0 + 2 + dyn
                    ff_load(layer, 1, c, 0, r0, u - 2)
                    ff_load(layer, 1, c, 1, r0 + 1, u - 1)
                    ff_load(layer, 2, c - 1, 0, r0, u)
                    ff_load(layer, 2, c - 1, 1, r0 + 1, u + 1)

                with sp.Fori(0, 6) as i:
                    pair(i + 1, i * 4)
                pair(7, 24)
                ff_load(layer, 2, 7, 0, r0, w0 + 28)
                ff_load(layer, 2, 7, 1, r0 + 1, w0 + 29)

            straight(6, loads_ff0)
            ff(0, loads_ff0, W_FF0)
            straight(loads_ff0 + 32, loads_ff1)
            ff(1, loads_ff1, W_FF1)
            for t in range(NTL):
                sp.wait_ge(s_res, RES["11"] + t + 1)
                sp.dma_start(out[0, P * t:P * t + P, :], h[:, t, :]).then_inc(s_out, 16)
            sp.wait_ge(s_out, 16 * NTL)

        def wait_raw(eng, r):
            if r < 6:
                eng.wait_ge(s_first[r], 16)
            else:
                eng.wait_ge(s_raw[r % 2], 16 * (r // 2 - 2))

        def raw_slot(w):
            r = raw_of_unit[w]
            return first_raw[r] if r < 6 else raw[r % 2]

        @block.tensor
        def _(pe):
            def transposes(name, parts):
                n = tg_index[name]
                wait_group_copied(pe, n - 4)
                for col, rows_, src in parts:
                    last = pe.transpose(ps[0:rows_, 512 * (4 + n % 4) + col:512 * (4 + n % 4) + col + P],
                                        src, ident)
                last.then_inc(s_tg, 1)

            def norm_transposes(tag, src, permuted=False):
                for k, s in norm_list(tag):
                    if tag.startswith("pre"):
                        pe.wait_ge(s_xn, XN[tag] + (NTL if s == 0 else NT))
                    transposes((tag, k, s), [(P * (t - tiles(s)[0]), P, src[:, t, P * k:P * k + P]) for t in tiles(s)])

            def gate_rows(tag, layer):
                for s in streams[layer]:
                    for half in range(2):
                        n = tg_index[tag, s, half]
                        pe.wait_ge(s_dg, dg_index[tag, s, half] + 1)
                        wait_group_copied(pe, n - 4)
                        pe.matmul(bank(4 + n % 4), ones, diag[:, :, :].rearrange("p a b -> p (a b)"),
                                  start=True, stop=True).then_inc(s_tg, 1)

            def three_pass(dst, lhs, rhs, first, last):
                pe.matmul(dst, lhs[0], rhs[0], start=first, stop=False)
                pe.matmul(dst, lhs[0], rhs[1], start=False, stop=False)
                return pe.matmul(dst, lhs[1], rhs[0], start=False, stop=last)

            def side_job(job):
                kind, a, t = job
                m = job_index[job]
                pe.wait_ge(s_jobf, m) if m else None
                if kind in ("ada", "flush"):
                    before = a if kind == "flush" else a - 1 if a not in (0, 8) else None
                    if before is not None:
                        for mt in range(2):
                            last = pe.transpose(bank(7)[:, UW + 4 * mt:UW + 4 * mt + 4],
                                                modrow[before % 2][0:4, P * mt:P * mt + P], ident[0:4, 0:4])
                    if kind == "ada":
                        w = ada_unit(a)
                        pe.wait_ge(s_lo, w + 1)
                        for k in range(KT):
                            for part in (whi, wlo):
                                last = pe.matmul(bank(7, UW, 4), silu4[:, k, :], part[w % 2][:, k, :],
                                                 start=(k == 0 and part is whi), stop=(k == KT - 1 and part is wlo))
                else:
                    s = t % 2
                    n = SEQ if s == 0 else CTX
                    if t < 2:
                        for k in range(2):
                            last = pe.matmul(bank(7, n, NOPE), wuq[:, k, QH * a:QH * a + NOPE], cqT[:, k, span(s)],
                                             start=(k == 0), stop=(k == 1))
                    else:
                        last = pe.matmul(bank(7, n, NOPE), wukv[:, P * a:P * a + NOPE], ckvT[:, span(s)],
                                         start=True, stop=True)
                last.then_inc(s_job, 1)

            def attention(layer):
                def scores(i):
                    sc, _, _ = step_info(layer, i)
                    kind, hd, t = steps[layer][i]
                    if kind == "mla" and t == 0:
                        pe.wait_ge(s_jobf, job_index["head", hd, 3] + 1)
                        pe.wait_ge(s_qr, hd + 1)
                    for m, (q, ks) in enumerate(sc):
                        s = s_first_[layer, i] + m
                        if s >= 2:
                            pe.wait_ge(s_ex, s - 1)
                        col = 0
                        for kk in ks:
                            n = int(np.prod(kk.shape[1:]))
                            last = pe.matmul(ps[:, 1024 * (s % 2) + col:1024 * (s % 2) + col + n], q, kk,
                                             start=True, stop=True)
                            col += n
                        last.then_inc(s_s, 1)

                def probs_t(i):
                    T = T0[layer] + i
                    kind = steps[layer][i][0]
                    s = s_first_[layer, i]
                    _, vals, _ = step_info(layer, i)
                    if kind == "diff":
                        pe.wait_ge(s_pc, i - 48 + 1)
                    else:
                        pe.wait_ge(s_ex, s + 1)
                    if T >= 1:
                        pe.wait_ge(s_pta, T)
                        pe.wait_ge(s_ptb, T)
                    half = len(vals) // 2
                    for k in range(len(vals)):
                        b, col = (4, P * k) if k < half else (5, P * (k - half))
                        last = pe.transpose(bank(b)[:, col:col + P], probs[layer][:, s % 4, P * k:P * k + P], ident)
                    last.then_inc(s_t, 1)

                def values(i):
                    T = T0[layer] + i
                    _, vals, _ = step_info(layer, i)
                    pe.wait_ge(s_pta, T + 1)
                    pe.wait_ge(s_ptb, T + 1)
                    if T >= 1:
                        pe.wait_ge(s_oe, T)
                    if layer == 1 and i == 32:
                        pe.wait_ge(s_band, 16 * 32)
                    for k, v in enumerate(vals):
                        last = pe.matmul(bank(6, v.shape[1]), pT[:, T % 2, k, :], v,
                                         start=(k == 0), stop=(k == len(vals) - 1))
                    last.then_inc(s_pv, 1)

                n = len(steps[layer])
                for i in range(n + 2):
                    if i < n:
                        scores(i)
                    if i >= 2:
                        values(i - 2)
                    if 1 <= i <= n:
                        probs_t(i - 1)
                    if layer == 0 and i < n:
                        for job in jobs[i]:
                            side_job(job)

            def out_transposes(layer):
                tag = f"out{layer}"
                pe.wait_ge(s_oe, T0[layer] + len(steps[layer]))
                if layer == 0:
                    pe.wait_ge(s_jobf, job_count)
                    pe.wait_ge(s_post, POST["diffnorm"] + 1)
                norm_transposes(tag, otok)

            def wait_split_activations(tag, k, both):
                pe.wait_ge(s_tlo, TS[tag] + (k + 1) * NSTREAM[tag])

            def product_tile(w, g, act, t, tag, first_of_phase):
                if g >= 4:
                    pe.wait_ge(s_gf, g - 3)
                a = slice(P * t, P * t + P)
                for k in range(KT):
                    if first_of_phase:
                        wait_split_activations(tag, k, True)
                    last = three_pass(bank(g % 4, UW), (act[0][:, k, a], act[1][:, k, a]),
                                      (whi[w % 2][:, k, :], wlo[w % 2][:, k, :]), k == 0, k == KT - 1)
                last.then_inc(s_g, 1)

            def ff(layer, w0):
                streams_ = streams[layer]
                nt = NT if layer == 0 else NTL
                n_f1, n_f2 = 2, nt

                f1_base = 0 if layer == 0 else 32
                f2_base = 0 if layer == 0 else 8 * 2 * NT

                def hidden(c_par, wpos, wdyn, m0, mdyn, first=False):
                    for half in range(2):
                        w = wpos + half
                        pe.wait_ge(s_lo, w + 1 + wdyn)
                        for mt in range(2):
                            m = m0 + 2 * half + mt
                            b = 4 + 2 * (m % 2)
                            if not (first and m - f1_base < 2):
                                pe.wait_ge(s_relu, m - 1 + mdyn)
                            for k in range(KT):
                                if first and half == 0 and mt == 0:
                                    wait_split_activations(f"pre{layer}1", k, True)
                                lw = (whi[w % 2][:, k, P * mt:P * mt + P], wlo[w % 2][:, k, P * mt:P * mt + P])
                                for wi, ai, st, sp_ in ((0, 0, k == 0, False), (0, 1, False, False),
                                                        (1, 0, False, k == KT - 1)):
                                    act = (ahi, alo)[ai]
                                    for s in streams_:
                                        last = pe.matmul(bank(b + s, SEQ if s == 0 else CTX), lw[wi],
                                                         act[:, k, span(s)], start=st, stop=sp_)
                            last.then_inc(s_f1, 1)

                def down(c_par, wpos, wdyn, mdone, mdyn, g0, gdyn, first=False):
                    pe.wait_ge(s_ulo, mdone + mdyn)
                    for half in range(2):
                        w = wpos + half
                        pe.wait_ge(s_lo, w + 1 + wdyn)
                        hi = whi[w % 2][:, :, :].rearrange("p k n -> p (k n)").rearrange("p (k n) -> p k n", n=512)
                        lo = wlo[w % 2][:, :, :].rearrange("p k n -> p (k n)").rearrange("p (k n) -> p k n", n=512)
                        for t in range(nt):
                            g = g0 + half * nt + t
                            if not (first and g - g0 < 4):
                                pe.wait_ge(s_f2f, g - 3 + gdyn)
                            a = slice(P * t, P * t + P)
                            for k in range(4):
                                u = 4 * c_par + k
                                last = three_pass(bank(g % 4), (uhi[:, u, a], ulo[:, u, a]),
                                                  (hi[:, k, :], lo[:, k, :]), k == 0, k == 3)
                            last.then_inc(s_f2, 1)

                per = 2 * nt
                hidden(0, w0, 0, f1_base, 0, first=True)
                hidden(1, w0 + 2, 0, f1_base + 4, 0)
                down(0, w0 + 4, 0, f1_base + 4, 0, f2_base, 0, first=True)
                with pe.Fori(0, 3) as i:
                    for p in range(2):
                        hidden(p, w0 + 6 + 4 * p, i * 8, f1_base + 8 + 4 * p, i * 8)
                        down(1 - p, w0 + 8 + 4 * p, i * 8, f1_base + 8 + 4 * p, i * 8,
                             f2_base + per * (p + 1), i * (2 * per))
                down(1, w0 + 30, 0, f1_base + 32, 0, f2_base + 7 * per, 0)

            pe.wait_ge(s_small, 64)
            pe.wait_ge(s_silu, 3)
            for a in range(8):
                side_job(("ada", a, 0))
            side_job(("flush", 7, 0))
            pe.wait_ge(s_jobf, 9)
            norm_transposes("pre00", xn)
            def in_groups(layer, u):
                for f, s in (inproj0 if layer == 0 else inproj1)[u]:
                    first = (f, s) == (0, 0)
                    if first:
                        base = POST["in0"] if layer == 0 else POST["in1"]
                        pe.wait_ge(s_post, base + u + 1)
                    name = (f"in{layer}", u, f, s)
                    if layer == 0 and u == 1 and f == 1:
                        parts = [(P * (t - tiles(s)[0]), 32, stage[:, 1, t, 128:160]) for t in tiles(s)]
                    else:
                        parts = [(P * (t - tiles(s)[0]), P, stage[:, u % 2, t, P * f:P * f + P]) for t in tiles(s)]
                    transposes(name, parts)

            def input_projection(layer, w0, g):
                n_units = 8 if layer == 0 else 9
                for u in range(n_units):
                    w = w0 + u
                    pe.wait_ge(s_lo, w + 1)
                    nt = NT if layer == 0 else in1_tiles[u]
                    for t in range(nt):
                        product_tile(w, g, (ahi, alo), t, f"pre{layer}0", u == 0 and t == 0)
                        g += 1
                    if u >= 1:
                        in_groups(layer, u - 1)
                in_groups(layer, n_units - 1)

            input_projection(0, W_IN0, G_IN0)
            pe.wait_ge(s_mlaw, 32)
            wait_group_copied(pe, tg_index["in0", 0, 1, 0])
            wait_group_copied(pe, tg_index["in0", 0, 1, 1])
            g = G_QR
            for t in range(NT):
                pe.wait_ge(s_gf, g - 3)
                for k in range(2):
                    rope_cols = wuq[:, k, :].rearrange("p (h c) -> p h c", c=QH)[:, :, NOPE:QH]
                    last = pe.matmul(bank(g % 4, UW), cqT[:, k, P * t:P * t + P], rope_cols, start=(k == 0), stop=(k == 1))
                last.then_inc(s_g, 1)
                g += 1
            for t in range(NT):
                pe.wait_ge(s_gf, g - 3)
                value_cols = wukv[:, :].rearrange("p (h c) -> p h c", c=P)[:, :, NOPE:P]
                pe.matmul(bank(g % 4), ckvT[:, P * t:P * t + P], value_cols, start=True, stop=True).then_inc(s_g, 1)
                g += 1
            pe.wait_ge(s_post, POST["qr"] + 1)
            for f in range(2):
                for s in (0, 1):
                    transposes(("qr", f, s), [(P * (t - tiles(s)[0]), P, stage[:, 0, t, P * f:P * f + P]) for t in tiles(s)])
            wait_groups_before(pe, tg_index["qr", 1, 1] + 1)
            pe.wait_ge(s_gf, G_OUT0)
            for t in range(4):
                side_job(("head", 0, t))
            attention(0)

            def output_projection(layer, w0, g):
                nt = NT if layer == 0 else NTL
                for u in range(4):
                    pe.wait_ge(s_lo, w0 + u + 1)
                    for t in range(nt):
                        product_tile(w0 + u, g, (uhi, ulo), t, f"out{layer}", u == 0 and t == 0)
                        g += 1

            out_transposes(0)
            gate_rows("gate00", 0)
            output_projection(0, W_OUT0, G_OUT0)
            norm_transposes("pre01", xn)
            gate_rows("gate01", 0)
            wait_groups_before(pe, tg_index["gate01", 1, 1] + 1)
            pe.wait_ge(s_gf, G_IN1)
            ff(0, W_FF0)
            norm_transposes("pre10", xn)
            pe.wait_ge(s_f2f, 8 * 2 * NT)
            input_projection(1, W_IN1, G_IN1)
            wait_groups_before(pe, tg_index["in1", 6, 1, 1] + 1)
            pe.wait_ge(s_gf, G_OUT1)
            attention(1)
            out_transposes(1)
            gate_rows("gate10", 1)
            output_projection(1, W_OUT1, G_OUT1)
            norm_transposes("pre11", xn)
            gate_rows("gate11", 1)
            wait_groups_before(pe, tg_index["gate11", 0, 1] + 1)
            pe.wait_ge(s_gf, G_END)
            ff(1, W_FF1)

        def group_out(name):
            tag = name[0]
            if tag in TS:
                k, s = name[1], name[2]
                n = SEQ if s == 0 else CTX
                dst = tmp[:, tg_index[name] % 4, 0:n]
                if tag.startswith("pre"):
                    layer, sub = int(tag[3]), int(tag[4])
                    return (dst, scl[:, layer, sub, k, s:s + 1],
                            mods[:, 48 * layer + 24 * sub + k, s:s + 1])
                if tag == "out0" and k >= 4:
                    return dst, subc[:, 0:1], None
                if tag == "out1" and k >= 4:
                    return dst.rearrange("p (r j c) -> p j r c", r=ROWS, j=CHUNKS), None, None
                return dst, None, None
            if tag.startswith("gate"):
                return gate[:, name[1], 512 * name[2]:512 * name[2] + 512], None, None
            if tag == "qr":
                return qrT[:, name[1], span(name[2])], MLA_SCALE, None
            u, f, s = name[1:]
            cols_ = span(s)
            if tag == "in0":
                if u == 0:
                    return cqT[:, f, cols_], colv[:, C_QG + f:C_QG + f + 1], None
                if u == 1:
                    return ((ckvT[:, cols_], colv[:, C_KG:C_KG + 1], None) if f == 0 else
                            (krT[0:32, cols_], None, None))
                if u < 4:
                    return dqz[:, 2 * (2 * (u - 2) + f), cols_], HEAD_SCALE, None
                return dkT[:, 2 * (u - 4) + f, cols_], None, None
            kind = ODD_KINDS[u]
            if kind == "gq":
                return gqz[:, 2 * (2 * u + f), cols_], HEAD_SCALE, None
            if kind == "gkv":
                return gkT[:, f, cols_], None, None
            if kind == "nq":
                return (nqz[:, 2 * (2 * (u - 3) + f), :].rearrange("p (j r c) -> p r j c", j=CHUNKS, r=ROWS),
                        HEAD_SCALE, None)
            return nkT[:, 2 * (u - 5) + f, cols_], None, None

        def is_query_pair(name):
            return (name[0] == "in0" and name[1] in (2, 3)) or (name[0] == "in1" and ODD_KINDS[name[1]] in ("gq", "nq"))

        def second_tile(name):
            u, f, s = name[1:]
            if name[0] == "in0":
                return dqz[:, 2 * (2 * (u - 2) + f) + 1, span(s)]
            if ODD_KINDS[u] == "gq":
                return gqz[:, 2 * (2 * u + f) + 1, :]
            return nqz[:, 2 * (2 * (u - 3) + f) + 1, :].rearrange("p (j r c) -> p r j c", j=CHUNKS, r=ROWS)

        def group_in(name, dst):
            n = tg_index[name]
            size = int(np.prod(dst.shape[1:]))
            src = bank(4 + n % 4, size, dst.shape[0])
            if len(dst.shape) > 2 and name[0] == "out1":
                src = src.rearrange("p (j r c) -> p j r c", j=CHUNKS, r=ROWS)
            elif len(dst.shape) > 2:
                src = src.rearrange("p (r j c) -> p r j c", j=CHUNKS, r=ROWS)
            return src

        def zeroed(eng, name):
            eng.wait_ge(s_zero, 2 if name[0] == "in0" else 6)

        def split_target(tag):
            return (ahi, alo) if tag.startswith("pre") else (uhi, ulo)

        def unit_end(w):
            if w < W_IN0:
                return s_job, w + 1
            if W_ADA <= w < W_OUT0:
                return s_job, job_index["ada", w - W_ADA + 8, 0] + 1
            if W_IN0 <= w < W_ADA:
                return s_g, G_IN0 + NT * (w - W_IN0 + 1)
            if W_OUT0 <= w < W_FF0:
                return s_g, G_OUT0 + NT * (w - W_OUT0 + 1)
            if W_IN1 <= w < W_OUT1:
                return s_g, G_IN1 + sum(in1_tiles[:w - W_IN1 + 1])
            if W_OUT1 <= w < W_FF1:
                return s_g, G_OUT1 + NTL * (w - W_OUT1 + 1)
            layer, w0 = (0, W_FF0) if w < W_IN1 else (1, W_FF1)
            q = w - w0
            nt = NT if layer == 0 else NTL
            f1b, f2b, per = (0, 0, 2 * nt) if layer == 0 else (32, 16 * NT, 2 * nt)
            if q < 2:
                return s_f1, f1b + 2 * (q + 1)
            if q >= 30:
                return s_f2, f2b + 7 * per + nt * (q - 29)
            c, pos = (q - 2) // 4 + 1, (q - 2) % 4
            if pos < 2:
                return s_f1, f1b + 4 * c + 2 * (pos + 1)
            return s_f2, f2b + per * (c - 1) + nt * (pos - 1)

        def steps_of_ff(layer):
            return (NT, 0, 0) if layer == 0 else (NTL, 32, 16 * NT)

        @block.scalar
        def _(act):
            ac = [0]

            def split_hi(w, dyn=0, dyn_end=0, dyn_raw=0):
                r = raw_of_unit[w]
                if r < 6:
                    act.wait_ge(s_first[r], 16)
                else:
                    act.wait_ge(s_raw[r % 2], 16 * (r // 2 - 2) + dyn_raw)
                if w >= 2:
                    end, value = unit_end(w - 2)
                    act.wait_ge(end, value + dyn_end)
                act.activation(whi[w % 2][:, :, :], raw_slot(w)[:, :, :], ACT.Copy).then_inc(s_hi, 1)

            def square_sums(count_, srcs, dst, before=None):
                for i, src in enumerate(srcs):
                    if before:
                        act.wait_ge(*before(i))
                    if count_ + i > 0:
                        act.wait_ge(s_sq, count_ + i)
                    act.activation(junk[:, 0:src.shape[1]], src, ACT.Square,
                                   accum_out=ss[:, dst + i:dst + i + 1]).then_inc(s_sq, 1)

            def copy_group(name):
                n = tg_index[name]
                if n % 2:
                    return
                act.wait_ge(s_tg, n + 1)
                dst, scale, bias = group_out(name)
                src = group_in(name, dst)
                if is_query_pair(name):
                    zeroed(act, name)
                    act.activation(dst[0:64], src[0:64], ACT.Copy, scale=scale)
                    ins = act.activation(second_tile(name)[64:P], src[64:P], ACT.Copy, scale=scale)
                elif bias is not None:
                    ins = act.activation(dst, src, ACT.Identity, bias=bias, scale=scale)
                elif scale is not None:
                    ins = act.activation(dst, src, ACT.Copy, scale=scale)
                else:
                    ins = act.activation(dst, src, ACT.Copy)
                ins.then_inc(s_tga, 1)

            def split_groups(tag):
                lst = norm_list(tag)
                hi, _ = split_target(tag)
                for j in range(len(lst) + 1):
                    if j < len(lst):
                        name = (tag,) + lst[j]
                        if tg_index[name] % 2 == 0:
                            if j >= 4:
                                act.wait_ge(s_tlo, TS[tag] + j - 3)
                            copy_group(name)
                    if j >= 1:
                        k, s = lst[j - 1]
                        n = tg_index[tag, k, s]
                        wait_group_copied(act, n)
                        width = SEQ if s == 0 else CTX
                        act.activation(hi[:, k, span(s)], tmp[:, n % 4, 0:width], ACT.Copy).then_inc(s_thi, 1)

            def side_copy(job):
                kind, a, t = job
                m = job_index[job]
                act.wait_ge(s_job, m + 1)
                if kind in ("ada", "flush"):
                    before = a if kind == "flush" else a - 1 if a not in (0, 8) else None
                    if before is not None:
                        ins = act.activation(mods4[:, 2 * before:2 * before + 2, :].rearrange("p a b -> p (a b)"),
                                             bank(7)[:, UW:UW + 8], ACT.Copy)
                    if kind == "ada":
                        ins = act.activation(modrow[a % 2][:, :], bank(7, UW, 4), ACT.Copy)
                    ins.then_inc(s_jobf, 1)
                else:
                    s = t % 2
                    n = SEQ if s == 0 else CTX
                    dst = (qslot if t < 2 else kslot)[0:NOPE, a % 2, span(s)]
                    act.activation(dst, bank(7, n, NOPE), ACT.Copy,
                                   scale=MLA_SCALE if t < 2 else 1.0).then_inc(s_jobf, 1)

            def input_projection(layer, w0, g):
                n_units = 8 if layer == 0 else 9
                groups_of = inproj0 if layer == 0 else inproj1
                for u in range(n_units):
                    if u + 1 < n_units or layer == 0:
                        split_hi(w0 + u + 1)
                    if u >= 2 and groups_of[u - 2]:
                        act.wait_ge(s_tg, tg_index[(f"in{layer}", u - 2) + groups_of[u - 2][-1]] + 1)
                    for t in range(NT if layer == 0 else in1_tiles[u]):
                        act.wait_ge(s_g, g + 1)
                        src = bank(g % 4, UW)
                        if layer == 0:
                            if u < 2:
                                width = UW if u == 0 else P
                                act.wait_ge(s_sq, SQ["cq"] + NT * u + t)
                                act.activation(junk2[:, 0:width], src[:, 0:width], ACT.Square,
                                               accum_out=ss[:, 8 * u + t:8 * u + t + 1]).then_inc(s_sq, 1)
                            width = 160 if u == 1 else UW
                            dst = (stage[:, u % 2, t, 0:width] if u < 6 else
                                   dv[:, t, UW * (u - 6):UW * (u - 6) + UW])
                            act.activation(dst, src[:, 0:width], ACT.Copy).then_inc(s_gf, 1)
                        else:
                            kind = ODD_KINDS[u]
                            if kind == "gkv":
                                act.activation(stage[:, u % 2, t, :].rearrange("p (g d c) -> p g d c", g=2, d=2),
                                               src[:, 0:P].rearrange("p (g c) -> p g c", g=2).unsqueeze(2)
                                               .broadcast_to([P, 2, 2, 64]), ACT.Copy)
                                act.activation(gv[:, t, :], src[:, P:UW], ACT.Copy).then_inc(s_gf, 1)
                            else:
                                dst = (nvc[:, t - NTL, UW * (u - 7):UW * (u - 7) + UW]
                                       if kind == "nv" and t >= NTL else stage[:, u % 2, t, :])
                                act.activation(dst, src, ACT.Copy).then_inc(s_gf, 1)
                        g += 1
                    if u >= 1:
                        for fs in groups_of[u - 1]:
                            copy_group((f"in{layer}", u - 1) + fs)
                for fs in groups_of[n_units - 1]:
                    copy_group((f"in{layer}", n_units - 1) + fs)

            def attention(layer):
                owner = {}
                for i in range(len(steps[layer])):
                    for m in range(2 if steps[layer][i][0] == "diff" else 1):
                        owner[s_first_[layer, i] + m] = i

                def probs_b(i):
                    T = T0[layer] + i
                    _, vals, _ = step_info(layer, i)
                    act.wait_ge(s_t, T + 1)
                    if T >= 2:
                        act.wait_ge(s_pv, T - 1)
                    half = len(vals) // 2
                    n = len(vals) - half
                    act.activation(pT[:, T % 2, half:len(vals), :].rearrange("p a b -> p (a b)"),
                                   bank(5, P * n), ACT.Copy).then_inc(s_ptb, 1)

                n = len(steps[layer])
                for i in range(n + 1):
                    if i < n:
                        sc, _, _ = step_info(layer, i)
                        for m, (q, ks) in enumerate(sc):
                            s = s_first_[layer, i] + m
                            width = sum(int(np.prod(k.shape[1:])) for k in ks)
                            act.wait_ge(s_mx, s + 1)
                            if s - 4 in owner:
                                j = owner[s - 4]
                                act.wait_ge(s_t, T0[layer] + j + 1)
                                if steps[layer][j][0] != "diff":
                                    act.wait_ge(s_oe, T0[layer] + j + 1)
                            act.activation(probs[layer][:, s % 4, 0:width], ps[:, 1024 * (s % 2):1024 * (s % 2) + width],
                                           ACT.Exp, bias=nmax[:, s % 4:s % 4 + 1], scale=1.0,
                                           accum_out=rsum[:, s % 4:s % 4 + 1]).then_inc(s_ex, 1)
                    if i >= 1:
                        probs_b(i - 1)
                    if layer == 0 and i < n:
                        for job in jobs[i]:
                            if job[0] == "ada":
                                split_hi(ada_unit(job[1]) + 1)
                            side_copy(job)

            def output_projection(layer, w0, g):
                nt = NT if layer == 0 else NTL
                for u in range(4):
                    split_hi(w0 + u + 1)
                    for t in range(nt):
                        act.wait_ge(s_g, g + 1)
                        act.activation(xn[:, t, UW * u:UW * u + UW], bank(g % 4, UW), ACT.Copy).then_inc(s_gf, 1)
                        g += 1
                        if u == 3:
                            square_sums(SQ[f"post{layer}0"] + t, [xn[:, t, :]], t,
                                        before=lambda i, g=g: (s_gf, g))

            def pre_squares(tag, nt, res):
                square_sums(SQ[tag], [h[:, t, :] for t in range(nt)], 8,
                            before=(lambda i: (s_res, res + i + 1)) if res is not None else (lambda i: (s_x, 32)))

            def ff(layer):
                nt, f1b, f2b = steps_of_ff(layer)
                w0 = W_FF0 if layer == 0 else W_FF1
                width = TOK if layer == 0 else SEQ
                per = 2 * nt

                def hidden(m, dyn, free):
                    act.wait_ge(s_f1, m + 1 + dyn)
                    if m - f1b >= 2:
                        act.wait_ge(s_rsq, m - 1 + dyn)
                    act.activation(relu[:, m % 2, 0:width], ps[:, 512 * (4 + 2 * (m % 2)):512 * (4 + 2 * (m % 2)) + width],
                                   ACT.Relu).then_inc(s_relu, 1)
                    act.wait_ge(s_rsq, m + 1 + dyn)
                    if free is not None:
                        act.wait_ge(s_f2, free)
                    act.activation(uhi[:, m % 8, 0:width], rsq[:, m % 2, 0:width], ACT.Copy).then_inc(s_uhi, 1)

                def step(c, i=0, n=0):
                    q = w0 + 2 + 4 * (c - 1)
                    f1d, f2d, rawd = i * (4 * n), i * (per * n), i * (32 * n)
                    for pos in range(4):
                        nxt = q + pos + 1
                        split_hi(nxt, 0, f1d if pos in (1, 2) or (pos == 0 and c == 1) else f2d, rawd)
                        if pos < 2:
                            for mt in range(2):
                                m = f1b + 4 * c + 2 * pos + mt
                                hidden(m, f1d, None if c < 2 else f2b + per * (c - 1) + f2d)

                split_hi(w0 + 1)
                for m in (0, 1):
                    hidden(f1b + m, 0, None)
                split_hi(w0 + 2)
                for m in (2, 3):
                    hidden(f1b + m, 0, None)
                step(1)
                with act.Fori(0, 3) as i:
                    step(2, i, 2)
                    step(3, i, 2)
                split_hi(w0 + 31)
                if layer == 0:
                    split_hi(W_IN1)
                done = f2b + 7 * per + nt
                square_sums(SQ[f"post{layer}1"], [xn[:, t, :] for t in range(nt)], 0,
                            before=lambda t: (s_f2f, done + t + 1))

            act.wait_ge(s_small, 64)
            act.activation(sexp[:, :], colv[:, C_C:C_C + 2 * KT], ACT.Exp, scale=-1.0).then_inc(s_ac, 1)
            act.wait_ge(s_vc, 1)
            act.activation(lamt[:, :], lamt[:, :], ACT.Exp).then_inc(s_ac, 1)
            split_hi(0)
            for a in range(2):
                split_hi(a + 1)
                side_copy(("ada", a, 0))
            pre_squares("pre00", NT, None)
            for a in range(2, 8):
                split_hi(a + 1)
                side_copy(("ada", a, 0))
            side_copy(("flush", 7, 0))
            act.wait_ge(s_mod, 1)
            split_groups("pre00")
            input_projection(0, W_IN0, G_IN0)
            for t in range(2 * NT):
                g = G_QR + t
                act.wait_ge(s_g, g + 1)
                if t < NT:
                    act.activation(stage[:, 0, t, :], bank(g % 4, UW), ACT.Copy).then_inc(s_gf, 1)
                else:
                    act.activation(vmla[:, t - NT, :], bank(g % 4), ACT.Copy).then_inc(s_gf, 1)
            for f in range(2):
                for s in (0, 1):
                    copy_group(("qr", f, s))
            for t in range(4):
                side_copy(("head", 0, t))
            attention(0)
            act.wait_ge(s_mod, 2)
            split_groups("out0")
            for s in streams[0]:
                for half in range(2):
                    copy_group(("gate00", s, half))
            output_projection(0, W_OUT0, G_OUT0)
            pre_squares("pre01", NT, RES["00"])
            split_groups("pre01")
            for s in streams[0]:
                for half in range(2):
                    copy_group(("gate01", s, half))
            ff(0)
            pre_squares("pre10", NT, RES["01"])
            split_groups("pre10")
            input_projection(1, W_IN1, G_IN1)
            attention(1)
            split_hi(W_OUT1)
            split_groups("out1")
            for half in range(2):
                copy_group(("gate10", 0, half))
            output_projection(1, W_OUT1, G_OUT1)
            pre_squares("pre11", NTL, RES["10"])
            split_groups("pre11")
            for half in range(2):
                copy_group(("gate11", 0, half))
            ff(1)

        @block.gpsimd
        def _(pool):
            def zero_halves(tiles_):
                pairs = tiles_[:, :, :].rearrange("p (f two) n -> p f two n", two=2)
                pool.memset(pairs[64:P, :, 0, :], 0.0).then_inc(s_zero, 1)
                pool.memset(pairs[0:64, :, 1, :], 0.0).then_inc(s_zero, 1)

            pool.wait_ge(s_xn, NT)
            zero_halves(dqz)
            pool.wait_ge(s_f2, 16 * NT)
            zero_halves(gqz)
            zero_halves(nqz)

        @block.vector
        def _(dve):
            vc = [0]
            posts = [0]

            def link(ins):
                vc[0] += 1
                ins.then_inc(s_vc, 1)
                dve.wait_ge(s_vc, vc[0])

            def split_lo(w, dyn=0):
                dve.wait_ge(s_hi, w + 1 + dyn)
                dve.tensor_tensor(wlo[w % 2][:, :, :], raw_slot(w)[:, :, :], whi[w % 2][:, :, :].bitcast(F32),
                                  ALU.subtract).then_inc(s_lo, 1)

            def rsqrt_chain(c0, n, width):
                v, a, y, c = chv[:, c0:c0 + n], cha[:, c0:c0 + n], chy[:, c0:c0 + n], chi[:, c0:c0 + n]
                link(dve.tensor_scalar(v, ss[:, c0:c0 + n], 1.0 / width, EPS, ALU.mult, ALU.add))
                link(dve.tensor_scalar(c, v.bitcast(I32), 1, None, ALU.arith_shift_right))
                link(dve.tensor_scalar(y.bitcast(I32), c, -1.0, float(0x5f3759df), ALU.mult, ALU.add))
                for it in range(3):
                    out_ = rstd[:, c0:c0 + n] if it == 2 else y
                    link(dve.tensor_tensor(a, y, y, ALU.mult))
                    link(dve.scalar_tensor_tensor(out=a, in0=a, scalar=-0.5, in1=v, op0=ALU.mult, op1=ALU.mult))
                    link(dve.scalar_tensor_tensor(out=out_, in0=a, scalar=1.5, in1=y, op0=ALU.add, op1=ALU.mult))

            def copy_group(name):
                n = tg_index[name]
                if n % 2 == 0:
                    return
                dve.wait_ge(s_tg, n + 1)
                dst, scale, bias = group_out(name)
                src = group_in(name, dst)
                if is_query_pair(name):
                    zeroed(dve, name)
                    dve.tensor_scalar(dst[0:64], src[0:64], scale, None, ALU.mult)
                    ins = dve.tensor_scalar(second_tile(name)[64:P], src[64:P], scale, None, ALU.mult)
                elif bias is not None:
                    ins = dve.tensor_scalar(dst, src, scale, bias, ALU.mult, ALU.add)
                elif scale is not None:
                    ins = dve.tensor_scalar(dst, src, scale, None, ALU.mult)
                else:
                    ins = dve.tensor_copy(dst, src)
                ins.then_inc(s_tgd, 1)

            def split_groups(tag):
                lst = norm_list(tag)
                hi, lo = split_target(tag)
                for j in range(len(lst) + 2):
                    if j < len(lst):
                        if j >= 4 and tg_index[(tag,) + lst[j]] % 2:
                            dve.wait_ge(s_tlo, TS[tag] + j - 3)
                        copy_group((tag,) + lst[j])
                    if j >= 2:
                        k, s = lst[j - 2]
                        n = tg_index[tag, k, s]
                        width = SEQ if s == 0 else CTX
                        dve.wait_ge(s_thi, TS[tag] + j - 1)
                        dve.tensor_tensor(lo[:, k, span(s)], tmp[:, n % 4, 0:width],
                                          hi[:, k, span(s)].bitcast(F32), ALU.subtract).then_inc(s_tlo, 1)

            def normalize(tag, layer_tiles):
                for b in range(layer_tiles // 2):
                    dve.wait_ge(s_sq, SQ[tag] + 2 * b + 2)
                    rsqrt_chain(8 + 2 * b, 2, D)
                    for t in (2 * b, 2 * b + 1):
                        dve.tensor_scalar(xn[:, t, :], h[:, t, :], rstd[:, 8 + t:9 + t], None,
                                          ALU.mult).then_inc(s_xn, 1)

            def residual(tag, nt, gtag):
                if tag == "00":
                    dve.wait_ge(s_x, 64)
                for s in streams[int(tag[0])]:
                    for half in range(2):
                        wait_group_copied(dve, tg_index[gtag, s, half])
                for b in range(nt // 2):
                    dve.wait_ge(s_sq, SQ["post" + tag] + 2 * b + 2)
                    rsqrt_chain(2 * b, 2, D)
                    for t in (2 * b, 2 * b + 1):
                        link(dve.scalar_tensor_tensor(out=xn[:, t, :], in0=xn[:, t, :], scalar=rstd[:, t:t + 1],
                                                      in1=gate[:, 0 if t < NTL else 1, :], op0=ALU.mult,
                                                      op1=ALU.mult))
                        dve.tensor_tensor(h[:, t, :], h[:, t, :], xn[:, t, :], ALU.add).then_inc(s_res, 1)

            def gate_diagonals(tag, layer, sub):
                for s in streams[layer]:
                    for half in range(2):
                        d = dg_index[tag, s, half]
                        if d >= 1:
                            before = [k for k, v in dg_index.items() if v == d - 1][0]
                            dve.wait_ge(s_tg, tg_index[before] + 1)
                        col = gcol[:, layer, sub, 4 * half:4 * half + 4, s]
                        dve.tensor_tensor(diag[:, :, :], ident.unsqueeze(1).broadcast_to([P, 4, P]),
                                          col.unsqueeze(2).broadcast_to([P, 4, P]), ALU.mult).then_inc(s_dg, 1)
                        copy_group((tag, s, half))

            def modulation(lo_, hi_):
                link(dve.tensor_tensor(mods[:, lo_:hi_, :], mods4[:, lo_:hi_, 0:2], mods4[:, lo_:hi_, 2:4], ALU.add))
                link(dve.tensor_tensor(mods[:, lo_:hi_, :], mods[:, lo_:hi_, :],
                                       colv[:, C_B + lo_:C_B + hi_].unsqueeze(2).broadcast_to([P, hi_ - lo_, 2]),
                                       ALU.add))

            def gain(layer, i):
                return colv[:, C_G + 32 * layer + 8 * i:C_G + 32 * layer + 8 * i + 8].unsqueeze(2).broadcast_to([P, KT, 2])

            def scale_columns(layer, sub):
                m0 = 48 * layer + 24 * sub + 8
                return dve.scalar_tensor_tensor(out=scl[:, layer, sub, :, :], in0=mods[:, m0:m0 + 8, :], scalar=1.0,
                                                in1=gain(layer, 2 * sub), op0=ALU.add, op1=ALU.mult)

            def gate_columns(layer, sub):
                m0 = 48 * layer + 24 * sub + 16
                return dve.tensor_tensor(gcol[:, layer, sub, :, :], mods[:, m0:m0 + 8, :], gain(layer, 2 * sub + 1),
                                         ALU.mult)

            def rope(sl, blocks, half, cos, sin):
                x4 = sl.rearrange("p (b t c) -> p b t c", b=blocks, t=2)
                dims = [list(d) for d in x4.ap]
                swapped = bass.AP(x4.tensor, x4.offset + half, [dims[0], [2 * half, blocks], [-half, 2], [1, half]])
                n = 2 * half * blocks
                v1 = rt1[:, 0:n].rearrange("p (b t c) -> p b t c", b=blocks, t=2)
                v2 = rt2[:, 0:n].rearrange("p (b t c) -> p b t c", b=blocks, t=2)
                cosb = cos.unsqueeze(1).unsqueeze(1).broadcast_to([P, blocks, 2, half])
                sinb = sin.rearrange("p (t c) -> p t c", t=2).unsqueeze(1).broadcast_to([P, blocks, 2, half])
                dve.tensor_tensor(v1, x4, cosb, ALU.mult).then_inc(s_vc, 1)
                vc[0] += 1
                link(dve.tensor_tensor(v2, swapped, sinb, ALU.mult))
                link(dve.tensor_tensor(sl, rt1[:, 0:n], rt2[:, 0:n], ALU.add))

            def stage_ready():
                dve.tensor_copy(token[:, :], ident[:, 0:1]).then_inc(s_post, 1)
                posts[0] += 1
                dve.wait_ge(s_post, posts[0])

            def head_rope(slot, t, blocks):
                rope(stage[:, slot, t, 0:64 * blocks], blocks, 32, tabs[:, t, T_CH:T_CH + 32],
                            tabs[:, t, T_SH:T_SH + 64])

            def mla_rope(sl, t, blocks):
                rope(sl, blocks, 16, tabs[:, t, T_CM:T_CM + 16], tabs[:, t, T_SM:T_SM + 32])

            def process_even(u):
                dve.wait_ge(s_gf, G_IN0 + NT * (u + 1))
                if u < 2:
                    width = UW if u == 0 else P
                    rsqrt_chain(8 * u, NT, width)
                    for t in range(NT):
                        dve.tensor_scalar(stage[:, u, t, 0:width], stage[:, u, t, 0:width],
                                          rstd[:, 8 * u + t:8 * u + t + 1], None, ALU.mult)
                    if u == 1:
                        for t in range(NTL):
                            mla_rope(stage[:, 1, t, P:P + ROPE], t, 1)
                else:
                    for t in range(NTL):
                        head_rope(u % 2, t, 4)
                stage_ready()

            def process_odd(u):
                kind = ODD_KINDS[u]
                nt = in1_tiles[u]
                dve.wait_ge(s_gf, G_IN1 + sum(in1_tiles[:u + 1]))
                if kind in ("gq", "gkv"):
                    nb = 4
                    w = 64 * nb
                    blocks = stage[:, u % 2, 0:nt, 0:w].rearrange("p t (b c) -> p t b c", c=64)
                    sq = sqj[:, 0:nt, 0:w].rearrange("p t (b c) -> p t b c", c=64)
                    sums = ss[:, 0:nt * nb].rearrange("p (t b) -> p t b", b=nb)
                    g0 = 256 if kind == "gq" else 320
                    gains = rowv[:, g0:g0 + 64].unsqueeze(1).broadcast_to([P, nb, 64])
                    link(dve.tensor_tensor(sq, blocks, blocks, ALU.mult))
                    link(dve.tensor_reduce(sums, sq, AX.X, ALU.add))
                    rsqrt_chain(0, nt * nb, 64)
                    factors = rstd[:, 0:nt * nb].rearrange("p (t b) -> p t b", b=nb).unsqueeze(3).broadcast_to([P, nt, nb, 64])
                    link(dve.tensor_tensor(blocks, blocks, factors, ALU.mult))
                    for t in range(nt):
                        one = stage[:, u % 2, t, 0:w].rearrange("p (b c) -> p b c", c=64)
                        ins = dve.tensor_tensor(one, one, gains, ALU.mult)
                        if t < nt - 1:
                            continue
                        link(ins)
                    for t in range(NTL):
                        head_rope(u % 2, t, nb)
                stage_ready()

            def input_projection(layer, w0):
                n_units = 8 if layer == 0 else 9
                groups_of = inproj0 if layer == 0 else inproj1
                for u in range(n_units):
                    if u + 1 < n_units or layer == 0:
                        split_lo(w0 + u + 1)
                    if u >= 1:
                        for fs in groups_of[u - 1]:
                            copy_group((f"in{layer}", u - 1) + fs)
                    if groups_of[u]:
                        (process_even if layer == 0 else process_odd)(u)
                for fs in groups_of[n_units - 1]:
                    copy_group((f"in{layer}", n_units - 1) + fs)

            def attention(layer):
                def maxima(i):
                    kind, hd, t = steps[layer][i]
                    sc, _, _ = step_info(layer, i)
                    for m, (q, ks) in enumerate(sc):
                        s = s_first_[layer, i] + m
                        width = sum(int(np.prod(k.shape[1:])) for k in ks)
                        src = ps[:, 1024 * (s % 2):1024 * (s % 2) + width]
                        dve.wait_ge(s_s, s + 1)
                        if kind == "na":
                            r = bias_raw[t]
                            if hd == 0:
                                wait_raw(dve, r)
                            link(dve.tensor_tensor(src[:, 0:UW], src[:, 0:UW], raw[r % 2][:, hd, :], ALU.add))
                        dve.tensor_reduce(nmax[:, s % 4:s % 4 + 1], src, AX.X, ALU.max,
                                          negate=True).then_inc(s_mx, 1)

                def combine(i):
                    _, vals, _ = step_info(layer, i)
                    s, w = s_first_[layer, i], P * len(vals)
                    a, b = s % 4, (s + 1) % 4
                    dve.wait_ge(s_ex, s + 2)
                    link(dve.reciprocal(rinv[:, a:b + 1], rsum[:, a:b + 1]))
                    link(dve.tensor_tensor(rinv[:, b:b + 1], rinv[:, b:b + 1], neglam[:, :], ALU.mult))
                    link(dve.tensor_scalar(probs[layer][:, a, 0:w], probs[layer][:, a, 0:w], rinv[:, a:a + 1], None, ALU.mult))
                    dve.scalar_tensor_tensor(out=probs[layer][:, a, 0:w], in0=probs[layer][:, b, 0:w], scalar=rinv[:, b:b + 1],
                                             in1=probs[layer][:, a, 0:w], op0=ALU.mult, op1=ALU.add).then_inc(s_pc, 1)

                def probs_a(i):
                    T = T0[layer] + i
                    _, vals, _ = step_info(layer, i)
                    dve.wait_ge(s_t, T + 1)
                    if T >= 2:
                        dve.wait_ge(s_pv, T - 1)
                    half = len(vals) // 2
                    dve.tensor_copy(pT[:, T % 2, 0:half, :].rearrange("p a b -> p (a b)"),
                                    bank(4, P * half)).then_inc(s_pta, 1)

                def output(i):
                    T = T0[layer] + i
                    kind = steps[layer][i][0]
                    _, vals, dst = step_info(layer, i)
                    s = s_first_[layer, i]
                    if kind != "diff":
                        link(dve.reciprocal(rinv[:, s % 4:s % 4 + 1], rsum[:, s % 4:s % 4 + 1]))
                    dve.wait_ge(s_pv, T + 1)
                    c0 = 0 if kind == "diff" else value_half(layer, i)
                    src = bank(6)[:, c0:c0 + dst.shape[1]]
                    if kind == "diff":
                        dve.tensor_copy(dst, src).then_inc(s_oe, 1)
                    else:
                        dve.tensor_scalar(dst, src, rinv[:, s % 4:s % 4 + 1], None, ALU.mult).then_inc(s_oe, 1)

                n = len(steps[layer])
                for i in range(n + 2):
                    if i < n:
                        maxima(i)
                        kind, hd, t = steps[layer][i]
                        if kind == "mla" and t == 1 and hd + 1 < MLA_H:
                            dve.wait_ge(s_s, s_first_[0, NT * hd])
                            rope_rows(hd + 1)
                    if i >= 2:
                        output(i - 2)
                    if 1 <= i <= n:
                        probs_a(i - 1)
                    if i < n and steps[layer][i][0] == "diff":
                        combine(i)
                    if layer == 0 and i < n:
                        for job in jobs[i]:
                            if job[0] == "ada":
                                split_lo(ada_unit(job[1]) + 1)

            def rope_rows(hd):
                r0 = ROPE * (hd % 4)
                dve.tensor_copy(qslot[NOPE:QH, hd % 2, :], qrT[r0:r0 + ROPE, hd // 4, :]).then_inc(s_qr, 1)

            def output_projection(layer, w0):
                for u in range(4):
                    split_lo(w0 + u + 1)

            def ff(layer):
                nt, f1b, f2b = steps_of_ff(layer)
                w0 = W_FF0 if layer == 0 else W_FF1
                width = TOK if layer == 0 else SEQ
                per = 2 * nt

                def hidden(m, dyn):
                    dve.wait_ge(s_relu, m + 1 + dyn)
                    if m - f1b >= 2:
                        dve.wait_ge(s_ulo, m - 1 + dyn)
                    dve.tensor_tensor(rsq[:, m % 2, 0:width], relu[:, m % 2, 0:width], relu[:, m % 2, 0:width],
                                      ALU.mult).then_inc(s_rsq, 1)
                    dve.wait_ge(s_uhi, m + 1 + dyn)
                    dve.tensor_tensor(ulo[:, m % 8, 0:width], rsq[:, m % 2, 0:width],
                                      uhi[:, m % 8, 0:width].bitcast(F32), ALU.subtract).then_inc(s_ulo, 1)

                def down(g, half, dyn, first=False):
                    for t in range(nt):
                        dve.wait_ge(s_f2, g + t + 1 + dyn)
                        dst = xn[:, t, 512 * half:512 * half + 512]
                        if first:
                            dve.tensor_copy(dst, bank((g + t) % 4)).then_inc(s_f2f, 1)
                        else:
                            dve.wait_ge(s_f2f, g + t - per + 1 + dyn)
                            dve.tensor_tensor(dst, dst, bank((g + t) % 4), ALU.add).then_inc(s_f2f, 1)

                def step(c, i=0, n=0, first=False):
                    q = w0 + 2 + 4 * (c - 1)
                    f1d, f2d = i * (4 * n), i * (per * n)
                    for pos in range(4):
                        split_lo(q + pos + 1, i * (4 * n))
                        if pos < 2:
                            for mt in range(2):
                                hidden(f1b + 4 * c + 2 * pos + mt, f1d)
                        else:
                            down(f2b + per * (c - 1) + nt * (pos - 2), pos - 2, f2d, first)

                split_lo(w0 + 1)
                for m in (0, 1):
                    hidden(f1b + m, 0)
                split_lo(w0 + 2)
                for m in (2, 3):
                    hidden(f1b + m, 0)
                step(1, first=True)
                with dve.Fori(0, 3) as i:
                    step(2, i, 2)
                    step(3, i, 2)
                split_lo(w0 + 31)
                down(f2b + 7 * per, 0, 0)
                if layer == 0:
                    split_lo(W_IN1)
                down(f2b + 7 * per + nt, 1, 0)

            dve.wait_ge(s_small, 64)
            lam4 = rowv[:, 0:256].rearrange("p (a b c) -> p a b c", a=2, b=2)
            prod = diag[:, 0, :].rearrange("p (a c) -> p a c", a=2)
            dve.tensor_tensor(prod, lam4[:, :, 0, :], lam4[:, :, 1, :], ALU.mult).then_inc(s_silu, 1)
            dve.wait_ge(s_silu, 1)
            link(dve.tensor_reduce(lamt[:, :], prod, AX.X, ALU.add))
            dve.wait_ge(s_ac, 1)
            link(dve.tensor_scalar(sexp[:, :], sexp[:, :], 1.0, None, ALU.add))
            link(dve.reciprocal(sexp[:, :], sexp[:, :]))
            dve.tensor_tensor(silu[:, :, :].rearrange("p a b -> p (a b)"), colv[:, C_C:C_C + 2 * KT], sexp[:, :],
                              ALU.mult).then_inc(s_silu, 1)
            dve.wait_ge(s_silu, 2)
            link(dve.tensor_copy(silu4[:, :, 0:2], silu[:, :, :]))
            dve.tensor_tensor(silu4[:, :, 2:4], silu[:, :, :], silu4[:, :, 0:2].bitcast(F32),
                              ALU.subtract).then_inc(s_silu, 1)
            dve.wait_ge(s_ac, 2)
            link(dve.tensor_tensor(neglam[:, :], lamt[:, 1:2], lamt[:, 0:1], ALU.subtract))
            link(dve.tensor_scalar(neglam[:, :], neglam[:, :], -LAM_INIT, None, ALU.add))
            link(dve.tensor_scalar(subc[:, :], colv[:, C_SUB:C_SUB + 1], 1.0 - LAM_INIT, None, ALU.mult))
            for w in range(3):
                split_lo(w)
            normalize("pre00", NT)
            for w in range(3, 9):
                split_lo(w)
            dve.wait_ge(s_jobf, 9)
            modulation(0, 16)
            scale_columns(0, 0).then_inc(s_mod, 1)
            dve.wait_ge(s_mod, 1)
            split_groups("pre00")
            input_projection(0, W_IN0)
            dve.wait_ge(s_gf, G_QR + NT)
            for t in range(NTL):
                mla_rope(stage[:, 0, t, :], t, MLA_H)
            stage_ready()
            for f in range(2):
                for s in (0, 1):
                    copy_group(("qr", f, s))
            wait_group_copied(dve, tg_index["in0", 1, 1, 0])
            wait_group_copied(dve, tg_index["in0", 1, 1, 1])
            wait_group_copied(dve, tg_index["qr", 1, 0])
            wait_group_copied(dve, tg_index["qr", 1, 1])
            for slot in range(2):
                dve.tensor_copy(kslot[NOPE:QH, slot, :], krT[0:ROPE, :])
            rope_rows(0)
            attention(0)
            dve.wait_ge(s_oe, n_steps0)
            for t in range(NT):
                o4 = otok[:, t, 512:1024].rearrange("p (b c) -> p b c", c=P)
                link(dve.tensor_tensor(tmp[:, 0, :].rearrange("p (b c) -> p b c", c=P), o4, o4, ALU.mult))
                link(dve.tensor_reduce(ss[:, 4 * t:4 * t + 4], tmp[:, 0, :].rearrange("p (b c) -> p b c", c=P),
                                       AX.X, ALU.add))
            rsqrt_chain(0, 24, P)
            for t in range(NT):
                o4 = otok[:, t, 512:1024].rearrange("p (b c) -> p b c", c=P)
                dve.tensor_tensor(o4, o4, rstd[:, 4 * t:4 * t + 4].unsqueeze(2).broadcast_to([P, 4, P]),
                                  ALU.mult)
            stage_ready()
            dve.wait_ge(s_jobf, job_count)
            modulation(16, 96)
            for layer, sub in ((0, 1), (1, 0), (1, 1)):
                link(scale_columns(layer, sub))
            for layer in range(2):
                for sub in range(2):
                    last = gate_columns(layer, sub)
            last.then_inc(s_mod, 1)
            dve.wait_ge(s_mod, 2)
            split_groups("out0")
            gate_diagonals("gate00", 0, 0)
            output_projection(0, W_OUT0)
            residual("00", NT, "gate00")
            normalize("pre01", NT)
            split_groups("pre01")
            gate_diagonals("gate01", 0, 1)
            ff(0)
            residual("01", NT, "gate01")
            normalize("pre10", NT)
            split_groups("pre10")
            input_projection(1, W_IN1)
            attention(1)
            split_lo(W_OUT1)
            split_groups("out1")
            gate_diagonals("gate10", 1, 0)
            output_projection(1, W_OUT1)
            residual("10", NTL, "gate10")
            normalize("pre11", NTL)
            split_groups("pre11")
            gate_diagonals("gate11", 1, 1)
            ff(1)
            residual("11", NTL, "gate11")


def shape_tables():
    t = np.arange(SEQ)
    row, col = (t // GRID_W).astype(np.float32), (t % GRID_W).astype(np.float32)
    parts = []
    for rot in (64, 32):
        n = rot // 4
        inv = (np.float32(10000.0) ** (-np.arange(n, dtype=np.float32) / np.float32(n))).astype(np.float32)
        ang = np.concatenate([row[:, None] * inv, col[:, None] * inv], axis=-1).astype(np.float32)
        parts += [np.cos(ang), -np.sin(ang), np.sin(ang)]
    return np.concatenate(parts, axis=-1).astype(np.float32)


def spread_bias(rpb):
    q, k = np.arange(P), np.arange(UW)
    r, c = q // CC, q % CC
    i, kc = k // BAND, k % BAND
    out = np.full((CHUNKS, P, 8, UW), -1e30, dtype=rpb.dtype)
    for j in range(CHUNKS):
        qcol = CC * j + c
        kcol = BAND_START[j] + kc
        start = np.clip(qcol - 8, 0, GRID_W - 16)
        seen = (kcol[None, :] >= start[:, None]) & (kcol[None, :] < start[:, None] + 16)
        rows_ = np.broadcast_to(i[None, :] - r[:, None] + 7, seen.shape)
        cols_ = np.clip(kcol[None, :] - qcol[:, None] + 15, 0, 30)
        for hd in range(8):
            out[j, :, hd, :][seen] = rpb[hd][rows_, cols_][seen]
    return out


def kernel(**inputs):
    import concourse.bacc as bacc
    from concourse.bass_utils import run_bass_kernel_spmd as run

    a = {k: np.asarray(v) for k, v in inputs.items()}
    per_partition = lambda v: np.moveaxis(v.reshape(v.shape[:-1] + (-1, P)), -1, 0).reshape(P, -1)
    cc = np.stack([a["c"][0], a["c_ctx"]], axis=-1).reshape(KT, P, 2)
    cols = np.concatenate([
        per_partition(a["norm_g"]), per_partition(a["b_ada"]), np.moveaxis(cc, 1, 0).reshape(P, -1),
        per_partition(a["mla_q_norm"][0]), per_partition(a["mla_kv_norm"][0]),
        per_partition(a["diff_subln"][0])], axis=1)
    rows = np.concatenate([a["diff_lambda"][0].reshape(-1), a["gqa_qk_norm"][0].reshape(-1)])
    consts = np.concatenate([np.eye(P), np.ones((P, P))], axis=1).astype(np.float32)
    arrays = {
        "x": a["x"], "ctx": a["ctx"], "cols": cols, "rows": rows, "consts": consts, "tables": shape_tables(),
        "na_bias": spread_bias(a["na_rpb"][0]), "w_ada": a["w_ada"], "w_ff1": a["w_ff1"], "w_ff2": a["w_ff2"],
        "w_in_even": a["w_in_even"], "w_out_even": a["w_out_even"], "w_uq": a["mla_w_uq"],
        "w_ukv": a["mla_w_ukv"], "w_in_odd": a["w_in_odd"], "w_out_odd": a["w_out_odd"]}
    nc = bacc.Bacc("TRN2", target_bir_lowering=False, num_devices=1, dynamic_dma_scratch_size=1024)
    feeds, args = {}, []
    for name, v in arrays.items():
        v = np.ascontiguousarray(v)
        feeds[f"in_{name}"] = v
        args.append(nc.dram_tensor(f"in_{name}", v.shape, mybir.dt.from_np(v.dtype), kind="ExternalInput").ap())
    args.append(nc.dram_tensor("out_h", (1, SEQ, D), F32, kind="ExternalOutput").ap())
    build(nc, *args)
    return run(nc, [feeds], core_ids=[0]).results[0]["out_h"]
```

```python
from contextlib import ExitStack

import numpy as np

import concourse.bass as bass
from concourse import mybir

F32 = mybir.dt.float32
F32R = mybir.dt.float32r
BF16 = mybir.dt.bfloat16
I32 = mybir.dt.int32
ALU = mybir.AluOpType
ACT = mybir.ActivationFunctionType
AX = mybir.AxisListType

P = 128
D = 1024
KT = D // P
SEQ, CTX = 512, 256
TOK = SEQ + CTX
NT, NTL = TOK // P, SEQ // P
DFF = 4 * D
GRID_W, ROWS = 64, 8
EPS = 1e-6
UW = 256
UE = KT * UW
MLA_H, NOPE, ROPE, QH = 8, 64, 32, 96
MLA_SCALE = float(QH) ** -0.5
HEAD_SCALE = 0.125
LAM_INIT = 0.8 - 0.6
CHUNKS, CC, BAND = 4, 16, 32
BAND_START = [min(max(CC * j - 8, 0), GRID_W - BAND) for j in range(CHUNKS)]
EVEN_STARTS = [0, 256, 416, 672, 928, 1184, 1440, 1696]
ODD_STARTS = [UW * u for u in range(9)]
ODD_KINDS = ["gq", "gq", "gkv", "nq", "nq", "nk", "nk", "nv", "nv"]
FF_CHUNKS = DFF // (2 * UW)
C_G, C_B, C_C, C_QG, C_KG, C_SUB, C_END = 0, 64, 160, 176, 178, 179, 180
K_ID, K_ONE, K_END = 0, 128, 256
T_CH, T_SH, T_CM, T_SM, T_END = 0, 32, 96, 112, 144


def attention_steps(layer):
    if layer == 0:
        return ([("mla", h, t) for h in range(MLA_H) for t in range(NT)]
                + [("diff", h, t) for h in range(4) for t in range(NT)])
    return ([("gqa", h, t) for h in range(8) for t in range(NTL)]
            + [("na", h, j) for j in range(CHUNKS) for h in range(8)])


def side_jobs():
    jobs, unit = [], 8
    for kind, h, t in attention_steps(0):
        here = []
        if kind == "mla" and h + 1 < MLA_H and t < 4:
            here.append(("head", h + 1, t))
        elif unit < 48:
            here.append(("ada", unit, 0))
            unit += 1
        jobs.append(here)
    jobs[-1].append(("flush", 47, 0))
    assert unit == 48
    return jobs


def build(nc, x, ctx, cols, rows, consts, tables, na_bias, w_ada, w_ff1, w_ff2, w_in_even,
          w_out_even, w_uq, w_ukv, w_in_odd, w_out_odd, out):
    steps = [attention_steps(0), attention_steps(1)]
    jobs = side_jobs()

    def win(w, c0):
        return w.rearrange("(k p) n -> p k n", p=P)[:, :, c0:c0 + UW]

    loads = [("s", win(w_ada[0], UW * a)) for a in range(8)]
    loads += [("s", win(w_in_even[0], c0)) for c0 in EVEN_STARTS]
    for here in jobs:
        loads += [("s", win(w_ada[a // 24], UW * (a % 24))) for kind, a, _ in here if kind == "ada"]
    loads += [("s", win(w_out_even[0], UW * u)) for u in range(4)]
    loads_ff0 = len(loads)
    loads += [("ff", None)] * 32
    loads += [("s", win(w_in_odd[0], c0)) for c0 in ODD_STARTS]
    loads += [("bias", na_bias[j].rearrange("p h k -> p (h k)")) for j in range(CHUNKS)]
    loads += [("s", win(w_out_odd[0], UW * u)) for u in range(4)]
    loads_ff1 = len(loads)
    loads += [("ff", None)] * 32

    with ExitStack() as stack:
        sem = lambda name: stack.enter_context(nc.semaphore(name))
        at = [1152]

        def place(name, shape, dt, offset=None):
            size = int(np.prod(shape[1:])) * (2 if dt == BF16 else 4)
            if offset is None:
                offset = at[0]
                at[0] += (size + 31) // 32 * 32
            return nc.alloc_sbuf_tensor_at(name, shape, dt, offset=offset)

        KB = 1024
        raw = [place(f"raw{i}", [P, KT, UW], F32) for i in range(2)]
        whi = [place(f"whi{i}", [P, KT, UW], F32R) for i in range(2)]
        wlo = [place(f"wlo{i}", [P, KT, UW], F32R) for i in range(2)]
        H = at[0]
        h = place("h", [P, NT, D], F32)
        dqz = place("dqz", [P, 8, TOK], F32, H)
        A = at[0]
        ahi = place("ahi", [P, KT, TOK], F32R)
        alo = place("alo", [P, KT, TOK], F32R)
        B = at[0]
        xn = place("xn", [P, NT, D], F32)
        C = at[0]
        uhi = place("uhi", [P, KT, TOK], F32R)
        ulo = place("ulo", [P, KT, TOK], F32R)
        whi += [place(f"first_whi{i}", [P, KT, UW], F32R, C + 16 * KB * i) for i in range(3)]
        wlo += [place(f"first_wlo{i}", [P, KT, UW], F32R, C + 16 * KB * i + 8 * KB) for i in range(3)]
        first_raw = [place(f"first_raw{i}", [P, KT, UW], F32, A + 8 * KB * i) for i in range(6)]
        otok = place("otok", [P, NT, D], F32, A)
        prob = place("prob", [P, 4, TOK], F32, A + 24 * KB)
        vmla = place("vmla", [P, NT, 512], F32, A + 36 * KB)
        cqT = place("cqT", [P, 2, TOK], F32, B)
        qrT = place("qrT", [P, 2, TOK], F32, B + 6 * KB)
        stage = place("stage", [P, 2, NT, UW], F32, B + 12 * KB)
        qslot = place("qslot", [P, 2, TOK], F32, B + 12 * KB)
        kslot = place("kslot", [P, 2, TOK], F32, B + 18 * KB)
        wuq = place("wuq", [P, 2, MLA_H * QH], F32, C)
        wukv = place("wukv", [P, MLA_H * P], F32, C + 6 * KB)
        dkT = place("dkT", [P, 4, TOK], F32, C + 10 * KB)
        dv = place("dv", [P, NT, 512], F32, C + 22 * KB)
        gkhi = place("gkhi", [P, 2, TOK], F32R, B)
        gklo = place("gklo", [P, 2, TOK], F32R, B + 6 * KB)
        gq2 = place("gq2", [P, 8, SEQ], F32R, C)
        gv = place("gv", [P, NT, P], F32, C + 44 * KB)
        nqz = place("nqz", [P, 8, SEQ], F32, C + 16 * KB)
        nkT = place("nkT", [P, 4, TOK], F32, C + 32 * KB)
        nvb = place("nvb", [P, CHUNKS, 2, 512], F32, A + 16 * KB)
        prob1 = place("prob1", [P, 4, TOK], F32, A + 36 * KB)
        G = at[0]
        gate = place("gate", [P, 2, D], F32)
        mods4 = place("mods4", [P, 96, 4], F32, G)
        S2 = at[0]
        relu = place("relu", [P, 2, TOK], F32)
        rsq = place("rsq", [P, 2, TOK], F32)
        tmp = place("tmp", [P, 4, 512], F32, S2)
        pT = place("pT", [P, 2, NT, P], F32, S2)
        sqj = place("sqj", [P, NT, UW], F32, S2)
        ckvT = place("ckvT", [P, TOK], F32, S2 + 6 * KB)
        nvc = place("nvc", [P, 2, 512], F32, S2 + 6 * KB)
        junk = place("junk", [P, D], BF16, S2 + 8 * KB)
        junk2 = place("junk2", [P, UW], BF16, S2 + 9 * KB)
        rt1 = place("rt1", [P, UW], F32, S2 + 10 * KB)
        rt2 = place("rt2", [P, UW], F32, S2 + 11 * KB)
        modrow = [place("modrow0", [4, UW], F32, S2 + 10 * KB), place("modrow1", [4, UW], F32, S2 + 11 * KB)]
        krT = place("krT", [32, TOK], F32)
        lam_prod = place("lam_prod", [P, P], F32, at[0] - 3 * KB)
        diag = place("diag", [P, 4, 4, P], F32, A)
        kons = place("kons", [P, K_END], F32)
        tabs = place("tabs", [P, NTL, T_END], F32)
        colv = place("colv", [P, C_END], F32)
        rowv = place("rowv", [P, 384], F32)
        mods = place("mods", [P, 96, 2], F32)
        scl = place("scl", [P, 2, 2, KT, 2], F32)
        gcol = place("gcol", [P, 2, 2, KT, 2], F32)
        silu = place("silu", [P, KT, 2], F32)
        silu4 = place("silu4", [P, KT, 4], F32R)
        sexp = place("sexp", [P, 2 * KT], F32)
        subc = place("subc", [P, 1], F32)
        lamt = place("lamt", [P, 2], F32)
        neglam = place("neglam", [P, 1], F32)
        ss = place("ss", [P, 24], F32)
        chv = place("chv", [P, 24], F32)
        pool_v = place("pool_v", [P, 2], F32)
        pool_a = place("pool_a", [P, 2], F32)
        pool_y = place("pool_y", [P, 2], F32)
        norm_rstd = place("norm_rstd", [P, 16], F32)
        cha = place("cha", [P, 24], F32)
        chy = place("chy", [P, 24], F32)
        rstd = place("rstd", [P, 24], F32)
        token = place("token", [P, 1], F32)
        nmax = place("nmax", [P, 4], F32)
        rsum = place("rsum", [P, 4], F32)
        rinv = place("rinv", [P, 4], F32)
        ratio = place("ratio", [P, 1], F32)
        assert at[0] <= 229344, at[0]
        ident = kons[:, K_ID:K_ID + P]
        ones = kons[:, K_ONE:K_ONE + P]
        ps = stack.enter_context(nc.psum_tensor("ps", [P, 8 * 512], F32))
        bank = lambda b, n=512, rows=P: ps[0:rows, 512 * b:512 * b + n]

        s_raw = [sem("raw_loaded0"), sem("raw_loaded1")]
        s_first = [sem(f"first_raw_loaded{i}") for i in range(6)]
        s_small = sem("small_loaded")
        s_x = [sem(f"x_loaded{b}") for b in range(NT // 2)]
        s_mlaw = sem("mla_weights_loaded")
        s_band = sem("band_values_moved")
        s_out = sem("out_stored")
        s_job = sem("side_job_done")
        s_tg = sem("transposes_done")
        s_g = sem("product_done")
        s_f1 = sem("hidden_done")
        s_f2 = sem("down_done")
        s_s = sem("scores_done")
        s_t = sem("probs_transposed")
        s_pv = sem("values_done")
        s_hi = sem("weights_hi_done")
        s_jobf = sem("side_job_copied")
        s_tga = sem("even_group_copied")
        s_gf = sem("product_copied")
        s_relu = sem("relu_done")
        s_uhi = sem("hidden_hi_done")
        s_thi = sem("activations_hi_done")
        s_sq = sem("squares_summed")
        s_xn = sem("normed")
        s_ex = sem("exp_done")
        s_ptb = sem("probs_b_copied")
        s_ac = sem("scalar_chain")
        s_hq = sem("query_or_key_hi_done")
        s_rstd = sem("rstd_ready")
        s_zero = sem("queries_zeroed")
        s_pool = sem("gpsimd_chain")
        s_lo = sem("weights_lo_done")
        s_tgd = sem("odd_group_copied")
        s_tlo = sem("activations_lo_done")
        s_res = sem("residual_added")
        s_rsq = sem("relu_squared")
        s_ulo = sem("hidden_lo_done")
        s_f2f = sem("down_added")
        s_mx = sem("max_done")
        s_pc = sem("diff_probs_combined")
        s_pta = sem("probs_a_copied")
        s_oe = sem("head_output_copied")
        s_dg = sem("gate_diagonal_done")
        s_post = sem("stage_processed")
        s_vc = sem("vector_chain")
        s_gated = sem("output_gated")
        s_qr = sem("rope_rows_copied")
        s_mod = sem("mods_ready")
        s_silu = sem("silu_ready")

        tg_index = {}
        tg_list = []

        def group(name):
            tg_index[name] = len(tg_list)
            tg_list.append(name)

        def norm_groups(tag, nt):
            for s in range(2 if nt > NTL else 1):
                for k in range(KT):
                    group((tag, k, s))

        streams = {0: (0, 1), 1: (0,)}
        norm_groups("pre00", NT)
        inproj0 = {u: ([(f, s) for f in range(2) for s in (0, 1)] if u not in (1, 6, 7) else
                       [(0, 0), (0, 1), (1, 0), (1, 1)] if u == 1 else []) for u in range(8)}
        for u in range(8):
            for fs in inproj0[u]:
                group(("in0", u) + fs)
        for fs in [(f, s) for f in range(2) for s in (0, 1)]:
            group(("qr",) + fs)
        norm_groups("out0", NT)
        for s in streams[0]:
            for half in range(2):
                group(("gate00", s, half))
        norm_groups("pre01", NT)
        for s in streams[0]:
            for half in range(2):
                group(("gate01", s, half))
        norm_groups("pre10", NT)
        inproj1 = {}
        for u, kind in enumerate(ODD_KINDS):
            both = (0,) if kind in ("gq", "nq") else (0, 1)
            inproj1[u] = [] if kind == "nv" else [(f, s) for f in range(2) for s in both]
            for fs in inproj1[u]:
                group(("in1", u) + fs)
        norm_groups("out1", NTL)
        for half in range(2):
            group(("gate10", 0, half))
        norm_groups("pre11", NTL)
        for half in range(2):
            group(("gate11", 0, half))

        def is_split_group(name):
            return (name[0] in ("out0", "out1")
                    or name[0] == "in1" and ODD_KINDS[name[1]] in ("gq", "gkv"))

        def copied_by_scalar(n):
            return n % 2 == 0 and not is_split_group(tg_list[n])

        def wait_group_copied(eng, n):
            if n < 0:
                return
            mine = copied_by_scalar(n)
            eng.wait_ge(s_tga if mine else s_tgd, sum(copied_by_scalar(i) == mine for i in range(n + 1)))

        def wait_groups_before(eng, n):
            for mine in (True, False):
                last = [i for i in range(n) if copied_by_scalar(i) == mine]
                if last:
                    wait_group_copied(eng, last[-1])

        def span(s):
            return slice(0, SEQ) if s == 0 else slice(SEQ, TOK)

        def tiles(s):
            return range(0, NTL) if s == 0 else range(NTL, NT)

        W_IN0, W_ADA, W_OUT0, W_FF0 = 8, 16, 56, 60
        W_IN1 = W_FF0 + 32
        W_OUT1 = W_IN1 + 9
        W_FF1 = W_OUT1 + 4
        G_IN0 = 0
        G_QR = G_IN0 + 8 * NT
        G_V = G_QR + NT
        G_OUT0 = G_V + NT
        G_IN1 = G_OUT0 + 4 * NT
        in1_tiles = [NTL if k in ("gq", "nq") else NT for k in ODD_KINDS]
        G_OUT1 = G_IN1 + sum(in1_tiles)
        G_END = G_OUT1 + 4 * NTL
        n_steps0 = len(steps[0])
        s_first_, count = {}, 0
        for layer in range(2):
            for i, st in enumerate(steps[layer]):
                s_first_[layer, i] = count
                count += 2 if st[0] == "diff" else 1
        S_TOTAL = count
        T0 = {0: 0, 1: n_steps0}
        raw_index = {"ff0": loads_ff0, "ff1": loads_ff1}
        raw_of_unit = [r for r, l in enumerate(loads) if l[0] in ("s", "ff")]
        ada_unit = lambda a: a if a < 8 else W_ADA + a - 8
        bias_raw = [r for r, l in enumerate(loads) if l[0] == "bias"]
        job_count = 8
        job_index = {("ada", a, 0): a for a in range(8)}
        job_index["flush", 7, 0] = job_count
        job_count += 1
        for t in range(4):
            job_index["head", 0, t] = job_count
            job_count += 1
        for here in jobs:
            for j in here:
                job_index[j] = job_count
                job_count += 1

        sq_index = {}
        sq_list = ([("pre00", t) for t in range(NT)] + [("cq", t) for t in range(NT)]
                   + [("ckv", t) for t in range(NT)] + [("diffnorm", i) for i in range(24)])
        for post, pre, nt in (("post00", "pre01", NT), ("post01", "pre10", NT), ("post10", "pre11", NTL),
                              ("post11", None, NTL)):
            for t in range(nt):
                sq_list.append((post, t))
                if pre and t % 2 == 0 and t:
                    sq_list += [(pre, t - 2), (pre, t - 1)]
            if pre:
                sq_list += [(pre, nt - 2), (pre, nt - 1)]
        for i, name in enumerate(sq_list):
            sq_index[name] = i
        rstd_index = {}
        for post, pre, nt in ((None, "pre00", NT), ("post00", "pre01", NT), ("post01", "pre10", NT),
                              ("post10", "pre11", NTL), ("post11", None, NTL)):
            for b in range(nt // 2):
                if post and b < nt // 2 - 1:
                    rstd_index[post, b] = len(rstd_index)
                if pre:
                    rstd_index[pre, b] = len(rstd_index)
        XN = {"pre00": 0, "pre01": 6, "pre10": 12, "pre11": 18}
        RES = {"00": 0, "01": 6, "10": 12, "11": 16}
        TS = {"pre00": 0, "pre01": 16, "pre10": 32, "pre11": 48}
        NSTREAM = {"pre00": 2, "out0": 2, "pre01": 2, "pre10": 2, "out1": 1, "pre11": 1}
        POST = {"in0": 0, "qr": 6, "diffnorm": 7, "in1": 9}

        dg_index = {}
        for tag, layer in (("gate00", 0), ("gate01", 0), ("gate10", 1), ("gate11", 1)):
            for s in streams[layer]:
                for half in range(2):
                    dg_index[tag, s, half] = len(dg_index)

        def norm_list(tag):
            return [(k, s) for s in range(NSTREAM[tag]) for k in range(KT)]

        def group_bank(name):
            n = tg_index[name]
            return n % 4 if name[0] in ("pre01", "pre11") else 4 + n % 4

        def step_info(layer, i):
            kind, hd, t = steps[layer][i]
            tcol = slice(P * t, P * t + P)
            keys = [(0, SEQ), (SEQ, TOK)] if (layer == 1 or t < NTL) else [(SEQ, TOK)]
            ktiles = list(range(NT)) if (layer == 1 or t < NTL) else list(range(NTL, NT))
            if kind == "mla":
                sc = [(qslot[0:QH, hd % 2, tcol], [kslot[0:QH, hd % 2, a:b] for a, b in keys])]
                vals = [vmla[:, k, P * (hd // 2):P * (hd // 2) + P] for k in ktiles]
                return sc, vals, otok[:, t, 64 * hd:64 * hd + 64]
            if kind == "diff":
                sc = [(dqz[:, 2 * hd + m, tcol], [dkT[:, hd, a:b] for a, b in keys]) for m in range(2)]
                vals = [dv[:, k, P * hd:P * hd + P] for k in ktiles]
                return sc, vals, otok[:, t, 512 + P * hd:512 + P * hd + P]
            if kind == "gqa":
                sc = [(gq2[:, hd, tcol], [(gkhi[:, hd // 4, a:b], gklo[:, hd // 4, a:b]) for a, b in keys])]
                vals = [gv[:, k, :] for k in ktiles]
                return sc, vals, otok[:, t, 64 * hd:64 * hd + 64]
            kk = nkT[:, hd // 2, 0:SEQ].rearrange("p (r c) -> p r c", c=GRID_W)
            b0 = BAND_START[t]
            sc = [(nqz[:, hd, tcol], [kk[:, :, b0:b0 + BAND], nkT[:, hd // 2, SEQ:TOK]])]
            pair = slice(P * (hd // 2), P * (hd // 2) + P)
            vals = [nvb[:, t, k, pair] for k in range(2)] + [nvc[:, k, pair] for k in range(2)]
            return sc, vals, otok[:, t, 512 + 64 * hd:512 + 64 * hd + 64]

        def width_of(kk):
            return int(np.prod((kk[0] if isinstance(kk, tuple) else kk).shape[1:]))

        def value_half(layer, i):
            kind, hd, _ = steps[layer][i]
            return 64 * (hd // 4 if kind == "gqa" else hd % 2)

        probs = [prob, prob1]

        block = stack.enter_context(nc.Block())

        @block.sync
        def _(sp):
            sp.dma_start(colv[:, :], cols).then_inc(s_small, 16)
            sp.dma_start(rowv[:, :], rows.partition_broadcast(P)).then_inc(s_small, 16)
            sp.dma_start(kons[:, :], consts).then_inc(s_small, 16)
            sp.dma_start(tabs[:, :, :], tables.rearrange("(t p) n -> p t n", p=P)).then_inc(s_small, 16)
            def load_h(batches):
                for b in batches:
                    src = x[0, 2 * P * b:2 * P * b + 2 * P] if b < NTL // 2 else ctx[0]
                    sp.dma_start(h[:, 2 * b:2 * b + 2, :], src.rearrange("(t p) d -> p t d", p=P)).then_inc(s_x[b], 16)

            load_h(range(NTL // 2))
            for r in range(6):
                sp.dma_start(first_raw[r][:, :, :], loads[r][1]).then_inc(s_first[r], 16)
            def slot_free(r):
                if loads[r][0] == "bias":
                    sp.wait_ge(s_mx, s_first_[1, 32 + 8 * bias_raw.index(r) + 7] + 1)
                else:
                    sp.wait_ge(s_lo, raw_of_unit.index(r) + 1)

            def ff_load(layer, kind, chunk, half, r, unit_before):
                if unit_before is not None:
                    sp.wait_ge(s_lo, unit_before + 1)
                if kind == 1:
                    src = w_ff1[layer].rearrange("(k p) n -> p k n", p=P)[
                        :, :, bass.ds(chunk * 512 + UW * half, UW)]
                    dst = raw[r % 2][:, :, :]
                else:
                    src = w_ff2[layer].rearrange("(c k p) n -> c p k n", p=P, k=4)[
                        bass.ds(chunk, 1), :, :, 512 * half:512 * half + 512].rearrange("c p k n -> p (c k) n")
                    dst = raw[r % 2][:, :, :].rearrange("p k n -> p (k n)").rearrange("p (k n) -> p k n", n=512)
                sp.dma_start(dst, src).then_inc(s_raw[r % 2], 16)

            def band_moves():
                sp.wait_ge(s_gf, G_OUT1)
                for u in (7, 8):
                    for j in range(CHUNKS):
                        for i in range(4):
                            src_p = GRID_W * (i % 2) + BAND_START[j]
                            src = stage[src_p:src_p + BAND, u % 2, i // 2:i // 2 + 3:2, :]
                            dst = nvb[BAND * i:BAND * i + BAND, j, :, UW * (u - 7):UW * (u - 7) + UW]
                            sp.dma_start(dst, src).then_inc(s_band, 16)

            def straight(r0, r1):
                for r in range(r0, r1):
                    kind, src = loads[r]
                    if kind == "bias" and r == bias_raw[0]:
                        band_moves()
                    if r >= 8:
                        slot_free(r - 2)
                    if r == W_OUT0 + 2:
                        sp.wait_ge(s_s, s_first_[1, 0])
                        load_h(range(NT // 2))
                    dst = raw[r % 2][:, :, :]
                    if kind == "bias":
                        dst = dst.rearrange("p k n -> p (k n)")
                    sp.dma_start(dst, src).then_inc(s_raw[r % 2], 16)

            def ff(layer, r0, w0):
                ff_load(layer, 1, 0, 0, r0, w0 - 2)
                ff_load(layer, 1, 0, 1, r0 + 1, w0 - 1)

                def pair(c, dyn):
                    u = w0 + 2 + dyn
                    ff_load(layer, 1, c, 0, r0, u - 2)
                    ff_load(layer, 1, c, 1, r0 + 1, u - 1)
                    ff_load(layer, 2, c - 1, 0, r0, u)
                    ff_load(layer, 2, c - 1, 1, r0 + 1, u + 1)

                with sp.Fori(0, 6) as i:
                    pair(i + 1, i * 4)
                pair(7, 24)
                ff_load(layer, 2, 7, 0, r0, w0 + 28)
                ff_load(layer, 2, 7, 1, r0 + 1, w0 + 29)

            straight(6, W_IN0)
            load_h([NT // 2 - 1])
            straight(W_IN0, W_IN0 + 2)
            sp.wait_ge(s_job, 8)
            sp.dma_start(wuq[:, :, :], w_uq[0].rearrange("(k p) n -> p k n", p=P)).then_inc(s_mlaw, 16)
            sp.dma_start(wukv[:, :], w_ukv[0]).then_inc(s_mlaw, 16)
            straight(W_IN0 + 2, loads_ff0)
            ff(0, loads_ff0, W_FF0)
            straight(loads_ff0 + 32, loads_ff1)
            ff(1, loads_ff1, W_FF1)
            for t in range(NTL):
                sp.wait_ge(s_res, RES["11"] + t + 1)
                sp.dma_start(out[0, P * t:P * t + P, :], h[:, t, :]).then_inc(s_out, 16)
            sp.wait_ge(s_out, 16 * NTL)

        def wait_raw(eng, r):
            if r < 6:
                eng.wait_ge(s_first[r], 16)
            else:
                eng.wait_ge(s_raw[r % 2], 16 * (r // 2 - 2))

        def wslot(w):
            return (2, 3, 4, 1, 0, 2, 3, 1)[w] if w < 8 else w % 2

        def unit_before(w):
            if w < 10:
                return {5: 0, 6: 1, 7: 3, 8: 4, 9: 7}.get(w)
            return w - 2

        def raw_slot(w):
            r = raw_of_unit[w]
            return first_raw[r] if r < 6 else raw[r % 2]

        @block.tensor
        def _(pe):
            def transposes(name, parts):
                wait_group_copied(pe, tg_index[name] - 4)
                for col, rows_, src in parts:
                    b = 512 * group_bank(name)
                    last = pe.transpose(ps[0:rows_, b + col:b + col + P], src, ident)
                last.then_inc(s_tg, 1)

            def norm_transposes(tag, k, s):
                src = xn if tag.startswith("pre") else otok
                if tag.startswith("pre"):
                    pe.wait_ge(s_xn, XN[tag] + (NTL if s == 0 else NT))
                if tag == "out0" and k == 4:
                    pe.wait_ge(s_post, POST["diffnorm"] + 1 + s)
                transposes((tag, k, s), [(P * (t - tiles(s)[0]), P, src[:, t, P * k:P * k + P]) for t in tiles(s)])

            def norm_phase(tag, product):
                order = norm_list(tag)
                done = 0
                for j in range(len(order) + (4 if len(order) == KT else 0)):
                    if tag == "out0" and j == 4:
                        while done < 4:
                            wait_split_activations(tag, done, 0)
                            product(done, 0)
                            done += 1
                    if j < len(order):
                        norm_transposes(tag, *order[j])
                    if done <= j - 4 < KT:
                        wait_split_activations(tag, done, 0)
                        product(done, 0)
                        done += 1
                if len(order) > KT:
                    for k in range(KT):
                        wait_split_activations(tag, k, 1)
                        product(k, 1)

            def first_products(w, g0, act, nt):
                def product(k, s):
                    pe.wait_ge(s_lo, w + 1)
                    for t in tiles(s):
                        if t >= nt:
                            continue
                        g = g0 + t
                        if k == 0 and g >= 4:
                            pe.wait_ge(s_gf, g - 3)
                        a = slice(P * t, P * t + P)
                        last = three_pass(bank(g % 4, UW), (act[0][:, k, a], act[1][:, k, a]),
                                          (whi[w % 2][:, k, :], wlo[w % 2][:, k, :]), k == 0, k == KT - 1)
                        if k == KT - 1:
                            last.then_inc(s_g, 1)
                return product

            def gate_rows(tag, layer):
                for s in streams[layer]:
                    for half in range(2):
                        n = tg_index[tag, s, half]
                        pe.wait_ge(s_dg, dg_index[tag, s, half] + 1)
                        wait_group_copied(pe, n - 4)
                        pe.matmul(bank(4 + n % 4), ones, diag[:, 2 * s + half, :, :].rearrange("p a b -> p (a b)"),
                                  start=True, stop=True).then_inc(s_tg, 1)

            def three_pass(dst, lhs, rhs, first, last):
                pe.matmul(dst, lhs[0], rhs[0], start=first, stop=False)
                pe.matmul(dst, lhs[0], rhs[1], start=False, stop=False)
                return pe.matmul(dst, lhs[1], rhs[0], start=False, stop=last)

            def side_job(job):
                kind, a, t = job
                m = job_index[job]
                pe.wait_ge(s_jobf, m) if m else None
                if kind in ("ada", "flush"):
                    before = a if kind == "flush" else a - 1 if a not in (0, 8) else None
                    if before is not None:
                        for mt in range(2):
                            last = pe.transpose(bank(7)[:, UW + 4 * mt:UW + 4 * mt + 4],
                                                modrow[before % 2][0:4, P * mt:P * mt + P], ident[0:4, 0:4])
                    if kind == "ada":
                        w = ada_unit(a)
                        pe.wait_ge(s_lo, w + 1)
                        for k in range(KT):
                            for part in (whi, wlo):
                                last = pe.matmul(bank(7, UW, 4), silu4[:, k, :], part[wslot(w)][:, k, :],
                                                 start=(k == 0 and part is whi), stop=(k == KT - 1 and part is wlo))
                else:
                    s = t % 2
                    n = SEQ if s == 0 else CTX
                    if t < 2:
                        for k in range(2):
                            last = pe.matmul(bank(7, n, NOPE), wuq[:, k, QH * a:QH * a + NOPE], cqT[:, k, span(s)],
                                             start=(k == 0), stop=(k == 1))
                    else:
                        last = pe.matmul(bank(7, n, NOPE), wukv[:, P * a:P * a + NOPE], ckvT[:, span(s)],
                                         start=True, stop=True)
                last.then_inc(s_job, 1)

            def attention(layer):
                def scores(i):
                    sc, _, _ = step_info(layer, i)
                    kind, hd, t = steps[layer][i]
                    if kind == "mla" and t == 0:
                        pe.wait_ge(s_jobf, job_index["head", hd, 3] + 1)
                        pe.wait_ge(s_qr, hd + 1)
                    for m, (q, ks) in enumerate(sc):
                        s = s_first_[layer, i] + m
                        if s >= 2:
                            pe.wait_ge(s_ex, s - 1)
                        col = 0
                        for kk in ks:
                            n = width_of(kk)
                            parts = kk if isinstance(kk, tuple) else (kk,)
                            for j, part in enumerate(parts):
                                last = pe.matmul(ps[:, 1024 * (s % 2) + col:1024 * (s % 2) + col + n], q, part,
                                                 start=(j == 0), stop=(j == len(parts) - 1))
                            col += n
                        last.then_inc(s_s, 1)

                def probs_t(i):
                    T = T0[layer] + i
                    kind = steps[layer][i][0]
                    s = s_first_[layer, i]
                    _, vals, _ = step_info(layer, i)
                    if kind == "diff":
                        pe.wait_ge(s_pc, i - 48 + 1)
                    else:
                        pe.wait_ge(s_ex, s + 1)
                    if T >= 1:
                        pe.wait_ge(s_pta, T)
                        pe.wait_ge(s_ptb, T)
                    half = len(vals) // 2
                    for k in range(len(vals)):
                        b, col = (4, P * k) if k < half else (5, P * (k - half))
                        last = pe.transpose(bank(b)[:, col:col + P], probs[layer][:, s % 4, P * k:P * k + P], ident)
                    last.then_inc(s_t, 1)

                def values(i):
                    T = T0[layer] + i
                    _, vals, _ = step_info(layer, i)
                    pe.wait_ge(s_pta, T + 1)
                    pe.wait_ge(s_ptb, T + 1)
                    if T >= 1:
                        pe.wait_ge(s_oe, T)
                    if layer == 1 and i == 32:
                        pe.wait_ge(s_band, 16 * 32)
                    for k, v in enumerate(vals):
                        last = pe.matmul(bank(6, v.shape[1]), pT[:, T % 2, k, :], v,
                                         start=(k == 0), stop=(k == len(vals) - 1))
                    last.then_inc(s_pv, 1)

                n = len(steps[layer])
                for i in range(n + 2):
                    if i < n:
                        scores(i)
                    if i >= 2 and layer == 0:
                        values(i - 2)
                    if 1 <= i <= n:
                        probs_t(i - 1)
                    if i >= 2 and layer == 1:
                        values(i - 2)
                    if layer == 0 and i < n:
                        for job in jobs[i]:
                            side_job(job)

            def wait_split_activations(tag, k, s):
                if tag in TS:
                    pe.wait_ge(s_tlo, TS[tag] + KT * s + k + 1)
                else:
                    wait_group_copied(pe, tg_index[tag, k, s])

            def product_tile(w, g, act, t):
                if g >= 4:
                    pe.wait_ge(s_gf, g - 3)
                a = slice(P * t, P * t + P)
                for k in range(KT):
                    last = three_pass(bank(g % 4, UW), (act[0][:, k, a], act[1][:, k, a]),
                                      (whi[w % 2][:, k, :], wlo[w % 2][:, k, :]), k == 0, k == KT - 1)
                last.then_inc(s_g, 1)

            def ff(layer, w0):
                streams_ = streams[layer]
                nt = NT if layer == 0 else NTL
                n_f1, n_f2 = 2, nt

                f1_base = 0 if layer == 0 else 32
                f2_base = 0 if layer == 0 else 8 * 2 * NT

                def first_hidden(w):
                    def product(k, s):
                        pe.wait_ge(s_lo, w + 1)
                        for mt in range(2):
                            last = three_pass(bank(4 + 2 * mt + s, SEQ if s == 0 else CTX),
                                              (whi[w % 2][:, k, P * mt:P * mt + P], wlo[w % 2][:, k, P * mt:P * mt + P]),
                                              (ahi[:, k, span(s)], alo[:, k, span(s)]), k == 0, k == KT - 1)
                            if s == streams_[-1] and k == KT - 1:
                                last.then_inc(s_f1, 1)

                    norm_phase(f"pre{layer}1", product)

                def hidden(c_par, wpos, wdyn, m0, mdyn, first=False):
                    for half in range(1 if first else 0, 2):
                        w = wpos + half
                        pe.wait_ge(s_lo, w + 1 + wdyn)
                        for mt in range(2):
                            m = m0 + 2 * half + mt
                            b = 4 + 2 * (m % 2)
                            pe.wait_ge(s_relu, m - 1 + mdyn)
                            for k in range(KT):
                                lw = (whi[w % 2][:, k, P * mt:P * mt + P], wlo[w % 2][:, k, P * mt:P * mt + P])
                                for wi, ai, st, sp_ in ((0, 0, k == 0, False), (0, 1, False, False),
                                                        (1, 0, False, k == KT - 1)):
                                    act = (ahi, alo)[ai]
                                    for s in streams_:
                                        last = pe.matmul(bank(b + s, SEQ if s == 0 else CTX), lw[wi],
                                                         act[:, k, span(s)], start=st, stop=sp_)
                            last.then_inc(s_f1, 1)

                def down(c_par, wpos, wdyn, mdone, mdyn, g0, gdyn, first=False):
                    pe.wait_ge(s_ulo, mdone + mdyn)
                    for half in range(2):
                        w = wpos + half
                        pe.wait_ge(s_lo, w + 1 + wdyn)
                        hi = whi[w % 2][:, :, :].rearrange("p k n -> p (k n)").rearrange("p (k n) -> p k n", n=512)
                        lo = wlo[w % 2][:, :, :].rearrange("p k n -> p (k n)").rearrange("p (k n) -> p k n", n=512)
                        for t in range(nt):
                            g = g0 + half * nt + t
                            if not (first and g - g0 < 4):
                                pe.wait_ge(s_f2f, g - 3 + gdyn)
                            a = slice(P * t, P * t + P)
                            for k in range(4):
                                u = 4 * c_par + k
                                last = three_pass(bank(g % 4), (uhi[:, u, a], ulo[:, u, a]),
                                                  (hi[:, k, :], lo[:, k, :]), k == 0, k == 3)
                            last.then_inc(s_f2, 1)

                def last_down(w, g0):
                    parts = [[m[w_ % 2][:, :, :].rearrange("p k n -> p (k n)").rearrange("p (k n) -> p k n", n=512)
                              for m in (whi, wlo)] for w_ in (w, w + 1)]
                    for t in range(nt):
                        for half in range(2):
                            g = g0 + 2 * t + half
                            if t == 0:
                                pe.wait_ge(s_lo, w + half + 1)
                            pe.wait_ge(s_f2f, g - 3)
                            a = slice(P * t, P * t + P)
                            for k in range(4):
                                last = three_pass(bank(g % 4), (uhi[:, 4 + k, a], ulo[:, 4 + k, a]),
                                                  (parts[half][0][:, k, :], parts[half][1][:, k, :]), k == 0, k == 3)
                            last.then_inc(s_f2, 1)

                per = 2 * nt
                first_hidden(w0)
                hidden(0, w0, 0, f1_base, 0, first=True)
                hidden(1, w0 + 2, 0, f1_base + 4, 0)
                down(0, w0 + 4, 0, f1_base + 4, 0, f2_base, 0, first=True)
                with pe.Fori(0, 3) as i:
                    for p in range(2):
                        hidden(p, w0 + 6 + 4 * p, i * 8, f1_base + 8 + 4 * p, i * 8)
                        down(1 - p, w0 + 8 + 4 * p, i * 8, f1_base + 8 + 4 * p, i * 8,
                             f2_base + per * (p + 1), i * (2 * per))
                pe.wait_ge(s_relu, f1_base + 32)
                gate_rows(f"gate{layer}1", layer)
                pe.wait_ge(s_ulo, f1_base + 32)
                last_down(w0 + 30, f2_base + 7 * per)

            pe.wait_ge(s_small, 64)
            pe.wait_ge(s_silu, 3)
            for a in range(8):
                side_job(("ada", a, 0))
            side_job(("flush", 7, 0))
            pe.wait_ge(s_jobf, 9)
            def in_groups(layer, u):
                for f, s in (inproj0 if layer == 0 else inproj1)[u]:
                    first = (f, s) == (0, 0)
                    if first:
                        base = POST["in0"] if layer == 0 else POST["in1"]
                        pe.wait_ge(s_post, base + u + 1)
                    name = (f"in{layer}", u, f, s)
                    if layer == 0 and u == 1 and f == 1:
                        parts = [(P * (t - tiles(s)[0]), 32, stage[:, 1, t, 128:160]) for t in tiles(s)]
                    else:
                        parts = [(P * (t - tiles(s)[0]), P, stage[:, u % 2, t, P * f:P * f + P]) for t in tiles(s)]
                    transposes(name, parts)

            def input_projection(layer, w0, g):
                n_units = 8 if layer == 0 else 9
                for u in range(n_units):
                    w = w0 + u
                    nt = NT if layer == 0 else in1_tiles[u]
                    if u == 0:
                        norm_phase(f"pre{layer}0", first_products(w, g, (ahi, alo), nt))
                        g += nt
                        continue
                    pe.wait_ge(s_lo, w + 1)
                    for t in range(nt):
                        product_tile(w, g, (ahi, alo), t)
                        g += 1
                    if u >= 1:
                        in_groups(layer, u - 1)
                in_groups(layer, n_units - 1)

            input_projection(0, W_IN0, G_IN0)
            pe.wait_ge(s_mlaw, 32)
            wait_group_copied(pe, tg_index["in0", 0, 1, 0])
            wait_group_copied(pe, tg_index["in0", 0, 1, 1])
            g = G_QR
            for t in range(NT):
                pe.wait_ge(s_gf, g - 3)
                for k in range(2):
                    rope_cols = wuq[:, k, :].rearrange("p (h c) -> p h c", c=QH)[:, :, NOPE:QH]
                    last = pe.matmul(bank(g % 4, UW), cqT[:, k, P * t:P * t + P], rope_cols, start=(k == 0), stop=(k == 1))
                last.then_inc(s_g, 1)
                g += 1
            for t in range(NT):
                pe.wait_ge(s_gf, g - 3)
                value_cols = wukv[:, :].rearrange("p (h c) -> p h c", c=P)[:, :, NOPE:P]
                pe.matmul(bank(g % 4), ckvT[:, P * t:P * t + P], value_cols, start=True, stop=True).then_inc(s_g, 1)
                g += 1
            pe.wait_ge(s_post, POST["qr"] + 1)
            for f in range(2):
                for s in (0, 1):
                    transposes(("qr", f, s), [(P * (t - tiles(s)[0]), P, stage[:, 0, t, P * f:P * f + P]) for t in tiles(s)])
            wait_groups_before(pe, tg_index["qr", 1, 1] + 1)
            pe.wait_ge(s_gf, G_OUT0)
            for t in range(4):
                side_job(("head", 0, t))
            attention(0)

            def output_projection(layer, w0, g):
                nt = NT if layer == 0 else NTL
                tag = f"out{layer}"
                pe.wait_ge(s_oe, T0[layer] + len(steps[layer]))
                if layer == 0:
                    pe.wait_ge(s_jobf, job_count)
                norm_phase(tag, first_products(w0, g, (uhi, ulo), nt))
                pe.wait_ge(s_lo, w0 + 2)
                g += nt
                for t in range(nt):
                    product_tile(w0 + 1, g, (uhi, ulo), t)
                    g += 1
                gate_rows(f"gate{layer}0", layer)
                for t in range(nt):
                    for u in (2, 3):
                        if t == 0:
                            pe.wait_ge(s_lo, w0 + u + 1)
                        product_tile(w0 + u, g, (uhi, ulo), t)
                        g += 1

            output_projection(0, W_OUT0, G_OUT0)
            pe.wait_ge(s_gf, G_IN1)
            wait_groups_before(pe, tg_index["gate00", 1, 1] + 1)
            ff(0, W_FF0)
            pe.wait_ge(s_f2f, 8 * 2 * NT)
            input_projection(1, W_IN1, G_IN1)
            wait_groups_before(pe, tg_index["in1", 6, 1, 1] + 1)
            pe.wait_ge(s_gf, G_OUT1)
            attention(1)
            output_projection(1, W_OUT1, G_OUT1)
            pe.wait_ge(s_gf, G_END)
            wait_groups_before(pe, tg_index["gate10", 0, 1] + 1)
            ff(1, W_FF1)

        def out_part(part, name):
            tag, k, s = name
            dst = part[:, k, span(s)]
            if tag == "out1" and k >= 4:
                return dst.rearrange("p (r j c) -> p j r c", r=ROWS, j=CHUNKS)
            return dst

        def group_out(name):
            tag = name[0]
            if tag in TS:
                k, s = name[1], name[2]
                n = SEQ if s == 0 else CTX
                layer, sub = int(tag[3]), int(tag[4])
                return (tmp[:, tg_index[name] % 4, 0:n], scl[:, layer, sub, k, s:s + 1],
                        mods[:, 48 * layer + 24 * sub + k, s:s + 1])
            if tag in ("out0", "out1"):
                return out_part(uhi, name), subc[:, 0:1] if tag == "out0" and name[1] >= 4 else None, None
            if tag.startswith("gate"):
                return gate[:, name[1], 512 * name[2]:512 * name[2] + 512], None, None
            if tag == "qr":
                return qrT[:, name[1], span(name[2])], MLA_SCALE, None
            u, f, s = name[1:]
            cols_ = span(s)
            if tag == "in0":
                if u == 0:
                    return cqT[:, f, cols_], colv[:, C_QG + f:C_QG + f + 1], None
                if u == 1:
                    return ((ckvT[:, cols_], colv[:, C_KG:C_KG + 1], None) if f == 0 else
                            (krT[0:32, cols_], None, None))
                if u < 4:
                    return dqz[:, 2 * (2 * (u - 2) + f), cols_], HEAD_SCALE, None
                return dkT[:, 2 * (u - 4) + f, cols_], None, None
            kind = ODD_KINDS[u]
            if kind == "gq":
                return gq2[:, 2 * (2 * u + f), cols_], HEAD_SCALE, None
            if kind == "gkv":
                return gkhi[:, f, cols_], None, None
            if kind == "nq":
                return (nqz[:, 2 * (2 * (u - 3) + f), :].rearrange("p (j r c) -> p r j c", j=CHUNKS, r=ROWS),
                        HEAD_SCALE, None)
            return nkT[:, 2 * (u - 5) + f, cols_], None, None

        def is_query_pair(name):
            return (name[0] == "in0" and name[1] in (2, 3)) or (name[0] == "in1" and ODD_KINDS[name[1]] == "nq")

        def second_tile(name):
            u, f, s = name[1:]
            if name[0] == "in0":
                return dqz[:, 2 * (2 * (u - 2) + f) + 1, span(s)]
            return nqz[:, 2 * (2 * (u - 3) + f) + 1, :].rearrange("p (j r c) -> p r j c", j=CHUNKS, r=ROWS)

        def group_in(name, dst):
            size = int(np.prod(dst.shape[1:]))
            src = bank(group_bank(name), size, dst.shape[0])
            if len(dst.shape) > 2 and name[0] == "out1":
                src = src.rearrange("p (j r c) -> p j r c", j=CHUNKS, r=ROWS)
            elif len(dst.shape) > 2:
                src = src.rearrange("p (r j c) -> p r j c", j=CHUNKS, r=ROWS)
            return src

        def zeroed(eng, name):
            eng.wait_ge(s_zero, 2 if name[0] == "in0" else 4)

        def unit_end(w):
            if w < W_IN0:
                return s_job, w + 1
            if W_ADA <= w < W_OUT0:
                return s_job, job_index["ada", w - W_ADA + 8, 0] + 1
            if W_IN0 <= w < W_ADA:
                return s_g, G_IN0 + NT * (w - W_IN0 + 1)
            if w in (W_OUT0 + 2, W_OUT0 + 3):
                return s_g, G_OUT0 + 4 * NT - 1 + (w - W_OUT0 - 2)
            if W_OUT0 <= w < W_FF0:
                return s_g, G_OUT0 + NT * (w - W_OUT0 + 1)
            if W_IN1 <= w < W_OUT1:
                return s_g, G_IN1 + sum(in1_tiles[:w - W_IN1 + 1])
            if w in (W_OUT1 + 2, W_OUT1 + 3):
                return s_g, G_OUT1 + 4 * NTL - 1 + (w - W_OUT1 - 2)
            if W_OUT1 <= w < W_FF1:
                return s_g, G_OUT1 + NTL * (w - W_OUT1 + 1)
            layer, w0 = (0, W_FF0) if w < W_IN1 else (1, W_FF1)
            q = w - w0
            nt = NT if layer == 0 else NTL
            f1b, f2b, per = (0, 0, 2 * nt) if layer == 0 else (32, 16 * NT, 2 * nt)
            if q < 2:
                return s_f1, f1b + 2 * (q + 1)
            if q >= 30:
                return s_f2, f2b + 8 * per - 1 + (q - 30)
            c, pos = (q - 2) // 4 + 1, (q - 2) % 4
            if pos < 2:
                return s_f1, f1b + 4 * c + 2 * (pos + 1)
            return s_f2, f2b + per * (c - 1) + nt * (pos - 1)

        def steps_of_ff(layer):
            return (NT, 0, 0) if layer == 0 else (NTL, 32, 16 * NT)

        @block.scalar
        def _(act):
            ac = [0]

            def split_hi(w, dyn=0, dyn_end=0, dyn_raw=0):
                r = raw_of_unit[w]
                if r < 6:
                    act.wait_ge(s_first[r], 16)
                else:
                    act.wait_ge(s_raw[r % 2], 16 * (r // 2 - 2) + dyn_raw)
                if unit_before(w) is not None:
                    end, value = unit_end(unit_before(w))
                    act.wait_ge(end, value + dyn_end)
                act.activation(whi[wslot(w)][:, :, :], raw_slot(w)[:, :, :], ACT.Copy).then_inc(s_hi, 1)

            def square_sum(name, src, col, scratch=None):
                i = sq_index[name]
                if i > 0:
                    act.wait_ge(s_sq, i)
                scratch = junk if scratch is None else scratch
                act.activation(scratch[:, 0:src.shape[1]], src, ACT.Square,
                               accum_out=ss[:, col:col + 1]).then_inc(s_sq, 1)

            def pre_squares(tag, b):
                for t in (2 * b, 2 * b + 1):
                    if tag == "pre00":
                        act.wait_ge(s_x[b], 16)
                    else:
                        act.wait_ge(s_res, RES[{"pre01": "00", "pre10": "01", "pre11": "10"}[tag]] + t + 1)
                    square_sum((tag, t), h[:, t, :], 8 + t)

            def normalize(tag, b):
                act.wait_ge(s_rstd, rstd_index[tag, b] + 1)
                for t in (2 * b, 2 * b + 1):
                    act.activation(xn[:, t, :], h[:, t, :], ACT.Copy, scale=norm_rstd[:, 8 + t:9 + t]).then_inc(s_xn, 1)

            def boundary(post, pre, nt, next_unit, product):
                for t in range(nt):
                    product(t, 0)
                    product(t, 1)
                    square_sum((post, t), xn[:, t, :], t)
                    if pre and t % 2 and t > 1:
                        normalize(pre, t // 2 - 1)
                    if t == nt - 1 and next_unit is not None:
                        split_hi(next_unit)
                    if pre and t % 2 == 0 and t:
                        pre_squares(pre, t // 2 - 1)
                if pre:
                    last = nt // 2 - 1
                    pre_squares(pre, last)
                    if nt > NTL:
                        split_groups(pre, 0, between=lambda: normalize(pre, last))
                        split_groups(pre, 1)
                    else:
                        normalize(pre, last)
                        split_groups(pre, 0)

            def copy_group(name):
                n = tg_index[name]
                if not copied_by_scalar(n) and not is_split_group(name):
                    return
                act.wait_ge(s_tg, n + 1)
                dst, scale, bias = group_out(name)
                src = group_in(name, dst)
                if is_split_group(name):
                    if name[0] != "in1":
                        act.activation(dst, src, ACT.Copy, scale=1.0 if scale is None else scale).then_inc(s_hq, 1)
                    elif ODD_KINDS[name[1]] == "gkv":
                        act.activation(dst, src, ACT.Copy).then_inc(s_hq, 1)
                    else:
                        e = 2 * (2 * name[1] + name[2])
                        act.activation(gq2[0:64, e, :], src[0:64], ACT.Copy, scale=scale)
                        act.activation(gq2[64:P, e + 1, :], src[64:P], ACT.Copy, scale=scale).then_inc(s_hq, 1)
                    return
                if is_query_pair(name):
                    zeroed(act, name)
                    act.activation(dst[0:64], src[0:64], ACT.Copy, scale=scale)
                    ins = act.activation(second_tile(name)[64:P], src[64:P], ACT.Copy, scale=scale)
                elif bias is not None:
                    ins = act.activation(dst, src, ACT.Identity, bias=bias, scale=scale)
                elif scale is not None:
                    ins = act.activation(dst, src, ACT.Copy, scale=scale)
                else:
                    ins = act.activation(dst, src, ACT.Copy)
                ins.then_inc(s_tga, 1)

            def split_groups(tag, s, between=None):
                for k in range(KT + 1):
                    if k == KT // 2 and between:
                        between()
                    if k < KT and copied_by_scalar(tg_index[tag, k, s]):
                        if k + KT * s >= 4:
                            act.wait_ge(s_tlo, TS[tag] + KT * s + k - 3)
                        copy_group((tag, k, s))
                    if k >= 1:
                        n = tg_index[tag, k - 1, s]
                        wait_group_copied(act, n)
                        width = SEQ if s == 0 else CTX
                        act.activation(ahi[:, k - 1, span(s)], tmp[:, n % 4, 0:width], ACT.Copy).then_inc(s_thi, 1)

            def side_copy(job):
                kind, a, t = job
                m = job_index[job]
                act.wait_ge(s_job, m + 1)
                if kind in ("ada", "flush"):
                    before = a if kind == "flush" else a - 1 if a not in (0, 8) else None
                    if before is not None:
                        ins = act.activation(mods4[:, 2 * before:2 * before + 2, :].rearrange("p a b -> p (a b)"),
                                             bank(7)[:, UW:UW + 8], ACT.Copy)
                    if kind == "ada":
                        ins = act.activation(modrow[a % 2][:, :], bank(7, UW, 4), ACT.Copy)
                    ins.then_inc(s_jobf, 1)
                else:
                    s = t % 2
                    n = SEQ if s == 0 else CTX
                    dst = (qslot if t < 2 else kslot)[0:NOPE, a % 2, span(s)]
                    act.activation(dst, bank(7, n, NOPE), ACT.Copy,
                                   scale=MLA_SCALE if t < 2 else 1.0).then_inc(s_jobf, 1)

            def input_projection(layer, w0, g):
                n_units = 8 if layer == 0 else 9
                groups_of = inproj0 if layer == 0 else inproj1
                for u in range(n_units):
                    if u + 1 < n_units or layer == 0:
                        split_hi(w0 + u + 1)
                    if u >= 2 and groups_of[u - 2]:
                        act.wait_ge(s_tg, tg_index[(f"in{layer}", u - 2) + groups_of[u - 2][-1]] + 1)
                    for t in range(NT if layer == 0 else in1_tiles[u]):
                        act.wait_ge(s_g, g + 1)
                        src = bank(g % 4, UW)
                        if layer == 0:
                            if u < 2:
                                width = UW if u == 0 else P
                                square_sum((("cq", "ckv")[u], t), src[:, 0:width], 8 * u + t, junk2)
                            width = 160 if u == 1 else UW
                            dst = (stage[:, u % 2, t, 0:width] if u < 6 else
                                   dv[:, t, UW * (u - 6):UW * (u - 6) + UW])
                            act.activation(dst, src[:, 0:width], ACT.Copy).then_inc(s_gf, 1)
                        else:
                            kind = ODD_KINDS[u]
                            if kind == "gkv":
                                act.activation(stage[:, u % 2, t, :].rearrange("p (g d c) -> p g d c", g=2, d=2),
                                               src[:, 0:P].rearrange("p (g c) -> p g c", g=2).unsqueeze(2)
                                               .broadcast_to([P, 2, 2, 64]), ACT.Copy)
                                act.activation(gv[:, t, :], src[:, P:UW], ACT.Copy).then_inc(s_gf, 1)
                            else:
                                dst = (nvc[:, t - NTL, UW * (u - 7):UW * (u - 7) + UW]
                                       if kind == "nv" and t >= NTL else stage[:, u % 2, t, :])
                                act.activation(dst, src, ACT.Copy).then_inc(s_gf, 1)
                        g += 1
                    if u >= 1:
                        for fs in groups_of[u - 1]:
                            copy_group((f"in{layer}", u - 1) + fs)
                for fs in groups_of[n_units - 1]:
                    copy_group((f"in{layer}", n_units - 1) + fs)

            def attention(layer):
                owner = {}
                for i in range(len(steps[layer])):
                    for m in range(2 if steps[layer][i][0] == "diff" else 1):
                        owner[s_first_[layer, i] + m] = i

                def probs_b(i):
                    T = T0[layer] + i
                    _, vals, _ = step_info(layer, i)
                    act.wait_ge(s_t, T + 1)
                    if T >= 2:
                        act.wait_ge(s_pv, T - 1)
                    half = len(vals) // 2
                    n = len(vals) - half
                    act.activation(pT[:, T % 2, half:len(vals), :].rearrange("p a b -> p (a b)"),
                                   bank(5, P * n), ACT.Copy).then_inc(s_ptb, 1)

                def diff_squares(i):
                    kind, hd, t = steps[layer][i]
                    if kind == "diff":
                        act.wait_ge(s_oe, T0[layer] + i + 1)
                        square_sum(("diffnorm", i - 48), otok[:, t, 512 + P * hd:512 + P * hd + P], 4 * t + hd, junk2)

                n = len(steps[layer])
                for i in range(n + 3):
                    if i >= 3:
                        diff_squares(i - 3)
                    if i > n:
                        continue
                    if layer == 1 and i == n - 4:
                        split_hi(W_OUT1)
                    if i < n:
                        sc, _, _ = step_info(layer, i)
                        for m, (q, ks) in enumerate(sc):
                            s = s_first_[layer, i] + m
                            width = sum(width_of(k) for k in ks)
                            act.wait_ge(s_mx, s + 1)
                            if s - 4 in owner:
                                j = owner[s - 4]
                                act.wait_ge(s_t, T0[layer] + j + 1)
                                if steps[layer][j][0] != "diff":
                                    act.wait_ge(s_oe, T0[layer] + j + 1)
                            act.activation(probs[layer][:, s % 4, 0:width], ps[:, 1024 * (s % 2):1024 * (s % 2) + width],
                                           ACT.Exp, bias=nmax[:, s % 4:s % 4 + 1], scale=1.0,
                                           accum_out=rsum[:, s % 4:s % 4 + 1]).then_inc(s_ex, 1)
                    if i >= 1:
                        probs_b(i - 1)
                    if layer == 0 and i < n:
                        for job in jobs[i]:
                            side_copy(job)
                            if job[0] == "ada" and ada_unit(job[1]) + 2 <= W_OUT0:
                                split_hi(ada_unit(job[1]) + 2)

            def output_projection(layer, w0, g0):
                nt = NT if layer == 0 else NTL

                def product(g, t, u):
                    act.wait_ge(s_g, g + 1)
                    act.activation(xn[:, t, UW * u:UW * u + UW], bank(g % 4, UW), ACT.Copy).then_inc(s_gf, 1)

                def product_of_pair(t, half):
                    g = g0 + 2 * nt + 2 * t + half
                    product(g, t, 2 + half)
                    if half:
                        act.wait_ge(s_gf, g + 1)

                for u in range(2):
                    if layer == 1 or u > 0:
                        split_hi(w0 + u + 1)
                    for t in range(nt):
                        product(g0 + nt * u + t, t, u)
                if layer == 0:
                    act.wait_ge(s_mod, 2)
                split_hi(w0 + 3)
                for s in streams[layer]:
                    for half in range(2):
                        copy_group((f"gate{layer}0", s, half))
                boundary(f"post{layer}0", f"pre{layer}1", nt, w0 + 4, product_of_pair)

            def ff(layer):
                nt, f1b, f2b = steps_of_ff(layer)
                w0 = W_FF0 if layer == 0 else W_FF1
                width = TOK if layer == 0 else SEQ
                per = 2 * nt

                def hidden(m, dyn, free):
                    act.wait_ge(s_f1, m + 1 + dyn)
                    if m - f1b >= 2:
                        act.wait_ge(s_rsq, m - 1 + dyn)
                    act.activation(relu[:, m % 2, 0:width], ps[:, 512 * (4 + 2 * (m % 2)):512 * (4 + 2 * (m % 2)) + width],
                                   ACT.Relu).then_inc(s_relu, 1)
                    act.wait_ge(s_rsq, m + 1 + dyn)
                    if free is not None:
                        act.wait_ge(s_f2, free)
                    act.activation(uhi[:, m % 8, 0:width], rsq[:, m % 2, 0:width], ACT.Copy).then_inc(s_uhi, 1)

                def step(c, i=0, n=0):
                    q = w0 + 2 + 4 * (c - 1)
                    f1d, f2d, rawd = i * (4 * n), i * (per * n), i * (32 * n)
                    for pos in range(4):
                        nxt = q + pos + 1
                        split_hi(nxt, 0, f1d if pos in (1, 2) or (pos == 0 and c == 1) else f2d, rawd)
                        if pos < 2:
                            for mt in range(2):
                                m = f1b + 4 * c + 2 * pos + mt
                                hidden(m, f1d, None if c < 2 else f2b + per * (c - 1) + f2d)

                split_hi(w0 + 1)
                for m in (0, 1):
                    hidden(f1b + m, 0, None)
                split_hi(w0 + 2)
                for m in (2, 3):
                    hidden(f1b + m, 0, None)
                step(1)
                with act.Fori(0, 3) as i:
                    step(2, i, 2)
                    step(3, i, 2)
                split_hi(w0 + 31)
                for s in streams[layer]:
                    for half in range(2):
                        copy_group((f"gate{layer}1", s, half))

                def summed(t, half):
                    if half:
                        act.wait_ge(s_f2f, f2b + 7 * per + 2 * t + 2)

                boundary(f"post{layer}1", "pre10" if layer == 0 else None, nt,
                         W_IN1 if layer == 0 else None, summed)

            act.wait_ge(s_small, 64)
            act.activation(sexp[:, :], colv[:, C_C:C_C + 2 * KT], ACT.Exp, scale=-1.0).then_inc(s_ac, 1)
            act.wait_ge(s_vc, 1)
            act.activation(lamt[:, :], lamt[:, :], ACT.Exp).then_inc(s_ac, 1)
            for b in range(NTL // 2):
                pre_squares("pre00", b)
            for w in range(3):
                split_hi(w)
            for a in range(8):
                side_copy(("ada", a, 0))
                if a + 3 < W_IN0:
                    split_hi(a + 3)
            side_copy(("flush", 7, 0))
            pre_squares("pre00", NT // 2 - 1)
            split_hi(W_IN0)
            act.wait_ge(s_mod, 1)
            split_groups("pre00", 0)
            split_groups("pre00", 1)
            input_projection(0, W_IN0, G_IN0)
            for t in range(2 * NT):
                g = G_QR + t
                act.wait_ge(s_g, g + 1)
                if t < NT:
                    act.activation(stage[:, 0, t, :], bank(g % 4, UW), ACT.Copy).then_inc(s_gf, 1)
                else:
                    act.activation(vmla[:, t - NT, :], bank(g % 4), ACT.Copy).then_inc(s_gf, 1)
            for f in range(2):
                for s in (0, 1):
                    copy_group(("qr", f, s))
            for t in range(4):
                side_copy(("head", 0, t))
            split_hi(W_ADA + 1)
            attention(0)
            for k, s in norm_list("out0"):
                if (k, s) == (4, 0):
                    split_hi(W_OUT0 + 1)
                copy_group(("out0", k, s))
            output_projection(0, W_OUT0, G_OUT0)
            ff(0)
            input_projection(1, W_IN1, G_IN1)
            attention(1)
            for k, s in norm_list("out1"):
                copy_group(("out1", k, s))
            output_projection(1, W_OUT1, G_OUT1)
            ff(1)

        @block.gpsimd
        def _(pool):
            def zero_halves(tiles_):
                pairs = tiles_[:, :, :].rearrange("p (f two) n -> p f two n", two=2)
                pool.memset(pairs[64:P, :, 0, :], 0.0).then_inc(s_zero, 1)
                pool.memset(pairs[0:64, :, 1, :], 0.0).then_inc(s_zero, 1)

            links = [0]

            def link(ins):
                links[0] += 1
                ins.then_inc(s_pool, 1)
                pool.wait_ge(s_pool, links[0])

            def chain(tag, b):
                pool.wait_ge(s_sq, sq_index[tag, 2 * b + 1] + 1)
                c0 = 2 * b + (8 if tag.startswith("pre") else 0)
                link(pool.tensor_scalar(pool_v[:, :], ss[:, c0:c0 + 2], 1.0 / D, EPS, ALU.mult, ALU.add))
                link(pool.tensor_scalar(pool_y[:, :].bitcast(I32), pool_v[:, :].bitcast(I32), -0.5,
                                        float(0x5f3759df), ALU.mult, ALU.add))
                for it in range(3):
                    link(pool.tensor_tensor(pool_a[:, :], pool_y[:, :], pool_y[:, :], ALU.mult))
                    link(pool.tensor_tensor(pool_a[:, :], pool_a[:, :], pool_v[:, :], ALU.mult))
                    link(pool.tensor_scalar(pool_a[:, :], pool_a[:, :], -0.5, 1.5, ALU.mult, ALU.add))
                    if it < 2:
                        link(pool.tensor_tensor(pool_y[:, :], pool_a[:, :], pool_y[:, :], ALU.mult))
                pool.tensor_tensor(norm_rstd[:, c0:c0 + 2], pool_a[:, :], pool_y[:, :],
                                   ALU.mult).then_inc(s_rstd, 1)
                pool.wait_ge(s_rstd, rstd_index[tag, b] + 1)

            for b in range(NT // 2):
                chain("pre00", b)
                for t in (2 * b, 2 * b + 1):
                    pool.tensor_scalar(xn[:, t, :], h[:, t, :], norm_rstd[:, 8 + t:9 + t], None,
                                       ALU.mult).then_inc(s_xn, 1)
            pool.wait_ge(s_xn, NT)
            zero_halves(dqz)
            for post, pre, nt in (("post00", "pre01", NT), ("post01", "pre10", NT)):
                for b in range(nt // 2):
                    if b < nt // 2 - 1:
                        chain(post, b)
                    chain(pre, b)
            pool.wait_ge(s_f2, 16 * NT)
            zero_halves(nqz)
            for tag in ("post10", "pre11", "post11"):
                for b in range(NTL // 2 - 1):
                    chain(tag, b)

        @block.vector
        def _(dve):
            vc = [0]
            posts = [0]

            def link(ins):
                vc[0] += 1
                ins.then_inc(s_vc, 1)
                dve.wait_ge(s_vc, vc[0])

            def split_lo(w, dyn=0):
                dve.wait_ge(s_hi, w + 1 + dyn)
                dve.tensor_tensor(wlo[wslot(w)][:, :, :], raw_slot(w)[:, :, :], whi[wslot(w)][:, :, :].bitcast(F32),
                                  ALU.subtract).then_inc(s_lo, 1)

            def rsqrt_chain(c0, n, width, dst=None, signal=False):
                v, a, y = chv[:, c0:c0 + n], cha[:, c0:c0 + n], chy[:, c0:c0 + n]
                link(dve.tensor_scalar(v, ss[:, c0:c0 + n], 1.0 / width, EPS, ALU.mult, ALU.add))
                link(dve.tensor_scalar(y.bitcast(I32), v.bitcast(I32), -0.5, float(0x5f3759df), ALU.mult, ALU.add))
                for it in range(3):
                    out_ = y if it < 2 else (rstd if dst is None else dst)[:, c0:c0 + n]
                    link(dve.tensor_tensor(a, y, y, ALU.mult))
                    link(dve.scalar_tensor_tensor(out=a, in0=a, scalar=-0.5, in1=v, op0=ALU.mult, op1=ALU.mult))
                    ins = dve.scalar_tensor_tensor(out=out_, in0=a, scalar=1.5, in1=y, op0=ALU.add, op1=ALU.mult)
                    if signal and it == 2:
                        ins.then_inc(s_rstd, 1)
                    else:
                        link(ins)

            def copy_group(name):
                n = tg_index[name]
                if copied_by_scalar(n):
                    return
                dve.wait_ge(s_tg, n + 1)
                dst, scale, bias = group_out(name)
                src = group_in(name, dst)
                if is_split_group(name):
                    dve.wait_ge(s_hq, sum(is_split_group(g) for g in tg_list[:n + 1]))
                    if name[0] != "in1" and scale is None:
                        ins = dve.tensor_tensor(out_part(ulo, name), src, dst.bitcast(F32), ALU.subtract)
                    elif name[0] != "in1":
                        ins = dve.scalar_tensor_tensor(out=out_part(ulo, name), in0=src, scalar=scale,
                                                       in1=dst.bitcast(F32), op0=ALU.mult, op1=ALU.subtract)
                    elif ODD_KINDS[name[1]] == "gkv":
                        ins = dve.tensor_tensor(gklo[:, name[2], span(name[3])], src, dst.bitcast(F32), ALU.subtract)
                    else:
                        e = 2 * (2 * name[1] + name[2])
                        dve.scalar_tensor_tensor(out=gq2[64:P, e, :], in0=src[0:64], scalar=scale,
                                                 in1=gq2[0:64, e, :].bitcast(F32), op0=ALU.mult, op1=ALU.subtract)
                        ins = dve.scalar_tensor_tensor(out=gq2[0:64, e + 1, :], in0=src[64:P], scalar=scale,
                                                       in1=gq2[64:P, e + 1, :].bitcast(F32), op0=ALU.mult,
                                                       op1=ALU.subtract)
                    ins.then_inc(s_tgd, 1)
                    return
                if is_query_pair(name):
                    zeroed(dve, name)
                    dve.tensor_scalar(dst[0:64], src[0:64], scale, None, ALU.mult)
                    ins = dve.tensor_scalar(second_tile(name)[64:P], src[64:P], scale, None, ALU.mult)
                elif bias is not None:
                    ins = dve.tensor_scalar(dst, src, scale, bias, ALU.mult, ALU.add)
                elif scale is not None:
                    ins = dve.tensor_scalar(dst, src, scale, None, ALU.mult)
                else:
                    ins = dve.tensor_copy(dst, src)
                ins.then_inc(s_tgd, 1)

            def split_groups(tag, s):
                for k in range(KT + 2):
                    if k < KT and not copied_by_scalar(tg_index[tag, k, s]):
                        if k + KT * s >= 4:
                            dve.wait_ge(s_tlo, TS[tag] + KT * s + k - 3)
                        copy_group((tag, k, s))
                    if k >= 2:
                        n = tg_index[tag, k - 2, s]
                        width = SEQ if s == 0 else CTX
                        dve.wait_ge(s_thi, TS[tag] + KT * s + k - 1)
                        dve.tensor_tensor(alo[:, k - 2, span(s)], tmp[:, n % 4, 0:width],
                                          ahi[:, k - 2, span(s)].bitcast(F32), ALU.subtract).then_inc(s_tlo, 1)

            def times_gate(post, t):
                dve.wait_ge(s_sq, sq_index[post, t] + 1)
                dve.tensor_tensor(xn[:, t, :], xn[:, t, :], gate[:, 0 if t < NTL else 1, :],
                                  ALU.mult).then_inc(s_gated, 1)

            def residual(post, b):
                res = RES[post[4:]]
                if (post, b) in rstd_index:
                    dve.wait_ge(s_rstd, rstd_index[post, b] + 1)
                else:
                    rsqrt_chain(2 * b, 2, D, norm_rstd)
                dve.wait_ge(s_gated, res + 2 * b + 2)
                for t in (2 * b, 2 * b + 1):
                    dve.scalar_tensor_tensor(out=h[:, t, :], in0=xn[:, t, :], scalar=norm_rstd[:, t:t + 1],
                                             in1=h[:, t, :], op0=ALU.mult, op1=ALU.add).then_inc(s_res, 1)

            def boundary(post, pre, nt, next_unit, product):
                for t in range(nt):
                    product(t)
                    if t == 0:
                        wait_groups_before(dve, tg_index["gate" + post[4:], 0 if nt == NTL else 1, 1] + 1)
                        if post == "post00":
                            for loaded in s_x:
                                dve.wait_ge(loaded, 32)
                    else:
                        times_gate(post, t - 1)
                    if t % 2 == 0 and t:
                        residual(post, t // 2 - 1)
                times_gate(post, nt - 1)
                residual(post, nt // 2 - 1)
                if next_unit is not None:
                    split_lo(next_unit)
                if pre:
                    if nt == NTL:
                        dve.wait_ge(s_sq, sq_index[pre, nt - 1] + 1)
                        rsqrt_chain(8 + nt - 2, 2, D, norm_rstd, signal=True)
                    for s in range(2 if nt > NTL else 1):
                        split_groups(pre, s)

            def gate_diagonals(tag, layer, sub):
                for s in streams[layer]:
                    for half in range(2):
                        col = gcol[:, layer, sub, 4 * half:4 * half + 4, s]
                        dve.tensor_tensor(diag[:, 2 * s + half, :, :], ident.unsqueeze(1).broadcast_to([P, 4, P]),
                                          col.unsqueeze(2).broadcast_to([P, 4, P]), ALU.mult).then_inc(s_dg, 1)

            def modulation(lo_, hi_):
                link(dve.tensor_tensor(mods[:, lo_:hi_, :], mods4[:, lo_:hi_, 0:2], mods4[:, lo_:hi_, 2:4], ALU.add))
                link(dve.tensor_tensor(mods[:, lo_:hi_, :], mods[:, lo_:hi_, :],
                                       colv[:, C_B + lo_:C_B + hi_].unsqueeze(2).broadcast_to([P, hi_ - lo_, 2]),
                                       ALU.add))

            def gain(layer, i):
                return colv[:, C_G + 32 * layer + 8 * i:C_G + 32 * layer + 8 * i + 8].unsqueeze(2).broadcast_to([P, KT, 2])

            def scale_columns(layer, sub):
                m0 = 48 * layer + 24 * sub + 8
                return dve.scalar_tensor_tensor(out=scl[:, layer, sub, :, :], in0=mods[:, m0:m0 + 8, :], scalar=1.0,
                                                in1=gain(layer, 2 * sub), op0=ALU.add, op1=ALU.mult)

            def gate_columns(layer, sub):
                m0 = 48 * layer + 24 * sub + 16
                return dve.tensor_tensor(gcol[:, layer, sub, :, :], mods[:, m0:m0 + 8, :], gain(layer, 2 * sub + 1),
                                         ALU.mult)

            def rope(sl, blocks, half, cos, sin):
                x4 = sl.rearrange("p (b t c) -> p b t c", b=blocks, t=2)
                dims = [list(d) for d in x4.ap]
                swapped = bass.AP(x4.tensor, x4.offset + half, [dims[0], [2 * half, blocks], [-half, 2], [1, half]])
                n = 2 * half * blocks
                v1 = rt1[:, 0:n].rearrange("p (b t c) -> p b t c", b=blocks, t=2)
                v2 = rt2[:, 0:n].rearrange("p (b t c) -> p b t c", b=blocks, t=2)
                cosb = cos.unsqueeze(1).unsqueeze(1).broadcast_to([P, blocks, 2, half])
                sinb = sin.rearrange("p (t c) -> p t c", t=2).unsqueeze(1).broadcast_to([P, blocks, 2, half])
                dve.tensor_tensor(v1, x4, cosb, ALU.mult).then_inc(s_vc, 1)
                vc[0] += 1
                link(dve.tensor_tensor(v2, swapped, sinb, ALU.mult))
                link(dve.tensor_tensor(sl, rt1[:, 0:n], rt2[:, 0:n], ALU.add))

            def stage_ready():
                dve.tensor_copy(token[:, :], ident[:, 0:1]).then_inc(s_post, 1)
                posts[0] += 1
                dve.wait_ge(s_post, posts[0])

            def head_rope(slot, t, blocks):
                rope(stage[:, slot, t, 0:64 * blocks], blocks, 32, tabs[:, t, T_CH:T_CH + 32],
                            tabs[:, t, T_SH:T_SH + 64])

            def mla_rope(sl, t, blocks):
                rope(sl, blocks, 16, tabs[:, t, T_CM:T_CM + 16], tabs[:, t, T_SM:T_SM + 32])

            def process_even(u):
                dve.wait_ge(s_gf, G_IN0 + NT * (u + 1))
                if u < 2:
                    width = UW if u == 0 else P
                    rsqrt_chain(8 * u, NT, width)
                    for t in range(NT):
                        dve.tensor_scalar(stage[:, u, t, 0:width], stage[:, u, t, 0:width],
                                          rstd[:, 8 * u + t:8 * u + t + 1], None, ALU.mult)
                    if u == 1:
                        for t in range(NTL):
                            mla_rope(stage[:, 1, t, P:P + ROPE], t, 1)
                else:
                    for t in range(NTL):
                        head_rope(u % 2, t, 4)
                stage_ready()

            def process_odd(u):
                kind = ODD_KINDS[u]
                nt = in1_tiles[u]
                dve.wait_ge(s_gf, G_IN1 + sum(in1_tiles[:u + 1]))
                if u == 0:
                    dve.wait_ge(s_tlo, TS["pre10"] + 2 * KT)
                if kind in ("gq", "gkv"):
                    nb = 4
                    w = 64 * nb
                    blocks = stage[:, u % 2, 0:nt, 0:w].rearrange("p t (b c) -> p t b c", c=64)
                    sq = sqj[:, 0:nt, 0:w].rearrange("p t (b c) -> p t b c", c=64)
                    sums = ss[:, 0:nt * nb].rearrange("p (t b) -> p t b", b=nb)
                    g0 = 256 if kind == "gq" else 320
                    gains = rowv[:, g0:g0 + 64].unsqueeze(1).broadcast_to([P, nb, 64])
                    link(dve.tensor_tensor(sq, blocks, blocks, ALU.mult))
                    link(dve.tensor_reduce(sums, sq, AX.X, ALU.add))
                    rsqrt_chain(0, nt * nb, 64)
                    factors = rstd[:, 0:nt * nb].rearrange("p (t b) -> p t b", b=nb).unsqueeze(3).broadcast_to([P, nt, nb, 64])
                    link(dve.tensor_tensor(blocks, blocks, factors, ALU.mult))
                    for t in range(nt):
                        one = stage[:, u % 2, t, 0:w].rearrange("p (b c) -> p b c", c=64)
                        ins = dve.tensor_tensor(one, one, gains, ALU.mult)
                        if t < nt - 1:
                            continue
                        link(ins)
                    for t in range(NTL):
                        head_rope(u % 2, t, nb)
                stage_ready()

            def input_projection(layer, w0):
                n_units = 8 if layer == 0 else 9
                groups_of = inproj0 if layer == 0 else inproj1
                for u in range(n_units):
                    if u + 1 < n_units or layer == 0:
                        split_lo(w0 + u + 1)
                    if u >= 1:
                        for fs in groups_of[u - 1]:
                            copy_group((f"in{layer}", u - 1) + fs)
                    if groups_of[u]:
                        (process_even if layer == 0 else process_odd)(u)
                for fs in groups_of[n_units - 1]:
                    copy_group((f"in{layer}", n_units - 1) + fs)

            def attention(layer):
                def maxima(i):
                    kind, hd, t = steps[layer][i]
                    sc, _, _ = step_info(layer, i)
                    for m, (q, ks) in enumerate(sc):
                        s = s_first_[layer, i] + m
                        width = sum(width_of(k) for k in ks)
                        src = ps[:, 1024 * (s % 2):1024 * (s % 2) + width]
                        dve.wait_ge(s_s, s + 1)
                        if kind == "na":
                            r = bias_raw[t]
                            if hd == 0:
                                wait_raw(dve, r)
                            link(dve.tensor_tensor(src[:, 0:UW], src[:, 0:UW], raw[r % 2][:, hd, :], ALU.add))
                        dve.tensor_reduce(nmax[:, s % 4:s % 4 + 1], src, AX.X, ALU.max,
                                          negate=True).then_inc(s_mx, 1)

                def combine(i):
                    _, vals, _ = step_info(layer, i)
                    s, w = s_first_[layer, i], P * len(vals)
                    a, b = s % 4, (s + 1) % 4
                    dve.wait_ge(s_ex, s + 2)
                    dve.wait_ge(s_oe, T0[layer] + i - 1)
                    link(dve.reciprocal(rinv[:, a:b + 1], rsum[:, a:b + 1]))
                    link(dve.tensor_scalar(ratio[:, :], rinv[:, b:b + 1], neglam[:, :], rsum[:, a:a + 1],
                                           ALU.mult, ALU.mult))
                    dve.scalar_tensor_tensor(out=prob[:, a, 0:w], in0=prob[:, b, 0:w], scalar=ratio[:, :],
                                             in1=prob[:, a, 0:w], op0=ALU.mult, op1=ALU.add).then_inc(s_pc, 1)

                def probs_a(i):
                    T = T0[layer] + i
                    _, vals, _ = step_info(layer, i)
                    dve.wait_ge(s_t, T + 1)
                    if T >= 2:
                        dve.wait_ge(s_pv, T - 1)
                    half = len(vals) // 2
                    dve.tensor_copy(pT[:, T % 2, 0:half, :].rearrange("p a b -> p (a b)"),
                                    bank(4, P * half)).then_inc(s_pta, 1)

                def output(i):
                    T = T0[layer] + i
                    kind = steps[layer][i][0]
                    _, vals, dst = step_info(layer, i)
                    s = s_first_[layer, i]
                    if kind != "diff":
                        link(dve.reciprocal(rinv[:, s % 4:s % 4 + 1], rsum[:, s % 4:s % 4 + 1]))
                    dve.wait_ge(s_pv, T + 1)
                    c0 = 0 if kind == "diff" else value_half(layer, i)
                    src = bank(6)[:, c0:c0 + dst.shape[1]]
                    dve.tensor_scalar(dst, src, rinv[:, s % 4:s % 4 + 1], None, ALU.mult).then_inc(s_oe, 1)

                n = len(steps[layer])
                for i in range(n + 2):
                    if i < n:
                        maxima(i)
                        kind, hd, t = steps[layer][i]
                        if kind == "mla" and t == 1 and hd + 1 < MLA_H:
                            dve.wait_ge(s_s, s_first_[0, NT * hd])
                            rope_rows(hd + 1)
                    if i >= 2 and layer == 0:
                        output(i - 2)
                    if 1 <= i <= n:
                        probs_a(i - 1)
                    if i >= 2 and layer == 1:
                        output(i - 2)
                    if layer == 0 and i < n:
                        for job in jobs[i]:
                            if job[0] == "ada":
                                split_lo(ada_unit(job[1]) + 1)
                    if i < n and steps[layer][i][0] == "diff":
                        combine(i)
                    if layer == 1 and i == n - 4:
                        split_lo(W_OUT1)

            def rope_rows(hd):
                r0 = ROPE * (hd % 4)
                dve.tensor_copy(qslot[NOPE:QH, hd % 2, :], qrT[r0:r0 + ROPE, hd // 4, :]).then_inc(s_qr, 1)

            def output_projection(layer, w0, g0):
                nt = NT if layer == 0 else NTL
                if layer == 1:
                    split_lo(w0 + 1)
                split_lo(w0 + 2)
                dve.wait_ge(s_g, g0 + nt)
                gate_diagonals(f"gate{layer}0", layer, 0)
                split_lo(w0 + 3)
                for s in streams[layer]:
                    for half in range(2):
                        copy_group((f"gate{layer}0", s, half))
                boundary(f"post{layer}0", f"pre{layer}1", nt, w0 + 4, lambda t: None)

            def ff(layer):
                nt, f1b, f2b = steps_of_ff(layer)
                w0 = W_FF0 if layer == 0 else W_FF1
                width = TOK if layer == 0 else SEQ
                per = 2 * nt

                def hidden(m, dyn):
                    dve.wait_ge(s_relu, m + 1 + dyn)
                    if m - f1b >= 2:
                        dve.wait_ge(s_ulo, m - 1 + dyn)
                    dve.tensor_tensor(rsq[:, m % 2, 0:width], relu[:, m % 2, 0:width], relu[:, m % 2, 0:width],
                                      ALU.mult).then_inc(s_rsq, 1)
                    dve.wait_ge(s_uhi, m + 1 + dyn)
                    dve.tensor_tensor(ulo[:, m % 8, 0:width], rsq[:, m % 2, 0:width],
                                      uhi[:, m % 8, 0:width].bitcast(F32), ALU.subtract).then_inc(s_ulo, 1)

                def down(g, half, dyn, first=False):
                    for t in range(nt):
                        dve.wait_ge(s_f2, g + t + 1 + dyn)
                        dst = xn[:, t, 512 * half:512 * half + 512]
                        if first:
                            dve.tensor_copy(dst, bank((g + t) % 4)).then_inc(s_f2f, 1)
                        else:
                            dve.wait_ge(s_f2f, g + t - per + 1 + dyn)
                            dve.tensor_tensor(dst, dst, bank((g + t) % 4), ALU.add).then_inc(s_f2f, 1)

                def step(c, i=0, n=0, first=False):
                    q = w0 + 2 + 4 * (c - 1)
                    f1d, f2d = i * (4 * n), i * (per * n)
                    for pos in range(4):
                        split_lo(q + pos + 1, i * (4 * n))
                        if pos < 2:
                            for mt in range(2):
                                hidden(f1b + 4 * c + 2 * pos + mt, f1d)
                        else:
                            down(f2b + per * (c - 1) + nt * (pos - 2), pos - 2, f2d, first)

                split_lo(w0 + 1)
                for m in (0, 1):
                    hidden(f1b + m, 0)
                split_lo(w0 + 2)
                for m in (2, 3):
                    hidden(f1b + m, 0)
                step(1, first=True)
                with dve.Fori(0, 3) as i:
                    step(2, i, 2)
                    step(3, i, 2)
                dve.wait_ge(s_f1, f1b + 32)
                gate_diagonals(f"gate{layer}1", layer, 1)
                split_lo(w0 + 31)
                for s in streams[layer]:
                    for half in range(2):
                        copy_group((f"gate{layer}1", s, half))

                def last_down(t):
                    for half in range(2):
                        g = f2b + 7 * per + 2 * t + half
                        dve.wait_ge(s_f2, g + 1)
                        dve.wait_ge(s_f2f, f2b + 6 * per + half * nt + t + 1)
                        dst = xn[:, t, 512 * half:512 * half + 512]
                        dve.tensor_tensor(dst, dst, bank(g % 4), ALU.add).then_inc(s_f2f, 1)

                boundary(f"post{layer}1", "pre10" if layer == 0 else None, nt,
                         W_IN1 if layer == 0 else None, last_down)

            dve.wait_ge(s_small, 64)
            lam4 = rowv[:, 0:256].rearrange("p (a b c) -> p a b c", a=2, b=2)
            prod = lam_prod[:, :].rearrange("p (a c) -> p a c", a=2)
            dve.tensor_tensor(prod, lam4[:, :, 0, :], lam4[:, :, 1, :], ALU.mult).then_inc(s_silu, 1)
            dve.wait_ge(s_silu, 1)
            link(dve.tensor_reduce(lamt[:, :], prod, AX.X, ALU.add))
            dve.wait_ge(s_ac, 1)
            link(dve.tensor_scalar(sexp[:, :], sexp[:, :], 1.0, None, ALU.add))
            link(dve.reciprocal(sexp[:, :], sexp[:, :]))
            dve.tensor_tensor(silu[:, :, :].rearrange("p a b -> p (a b)"), colv[:, C_C:C_C + 2 * KT], sexp[:, :],
                              ALU.mult).then_inc(s_silu, 1)
            dve.wait_ge(s_silu, 2)
            link(dve.tensor_copy(silu4[:, :, 0:2], silu[:, :, :]))
            dve.tensor_tensor(silu4[:, :, 2:4], silu[:, :, :], silu4[:, :, 0:2].bitcast(F32),
                              ALU.subtract).then_inc(s_silu, 1)
            dve.wait_ge(s_ac, 2)
            link(dve.tensor_tensor(neglam[:, :], lamt[:, 1:2], lamt[:, 0:1], ALU.subtract))
            link(dve.tensor_scalar(neglam[:, :], neglam[:, :], -LAM_INIT, None, ALU.add))
            link(dve.tensor_scalar(subc[:, :], colv[:, C_SUB:C_SUB + 1], 1.0 - LAM_INIT, None, ALU.mult))
            for w in range(8):
                split_lo(w)
            dve.wait_ge(s_jobf, 9)
            modulation(0, 16)
            scale_columns(0, 0).then_inc(s_mod, 1)
            dve.wait_ge(s_mod, 1)
            split_lo(W_IN0)
            split_groups("pre00", 0)
            split_groups("pre00", 1)
            input_projection(0, W_IN0)
            dve.wait_ge(s_gf, G_QR + NT)
            for t in range(NTL):
                mla_rope(stage[:, 0, t, :], t, MLA_H)
            stage_ready()
            for f in range(2):
                for s in (0, 1):
                    copy_group(("qr", f, s))
            wait_group_copied(dve, tg_index["in0", 1, 1, 0])
            wait_group_copied(dve, tg_index["in0", 1, 1, 1])
            wait_group_copied(dve, tg_index["qr", 1, 0])
            wait_group_copied(dve, tg_index["qr", 1, 1])
            for slot in range(2):
                dve.tensor_copy(kslot[NOPE:QH, slot, :], krT[0:ROPE, :])
            rope_rows(0)
            attention(0)
            def diff_norm(s):
                if s == 0:
                    dve.wait_ge(s_sq, sq_index["diffnorm", 23] + 1)
                    rsqrt_chain(0, 24, P)
                for t in tiles(s):
                    o4 = otok[:, t, 512:1024].rearrange("p (b c) -> p b c", c=P)
                    dve.tensor_tensor(o4, o4, rstd[:, 4 * t:4 * t + 4].unsqueeze(2).broadcast_to([P, 4, P]),
                                      ALU.mult)
                stage_ready()

            def later_modulation():
                dve.wait_ge(s_jobf, job_count)
                modulation(16, 96)
                for layer, sub in ((0, 1), (1, 0), (1, 1)):
                    link(scale_columns(layer, sub))
                for layer in range(2):
                    for sub in range(2):
                        last = gate_columns(layer, sub)
                last.then_inc(s_mod, 1)
                dve.wait_ge(s_mod, 2)

            for k, s in norm_list("out0"):
                if (k, s) == (4, 0):
                    diff_norm(0)
                if (k, s) == (0, 1):
                    diff_norm(1)
                    split_lo(W_OUT0 + 1)
                copy_group(("out0", k, s))
                if (k, s) == (6, 0):
                    later_modulation()
            output_projection(0, W_OUT0, G_OUT0)
            ff(0)
            input_projection(1, W_IN1)
            attention(1)
            for k, s in norm_list("out1"):
                copy_group(("out1", k, s))
            output_projection(1, W_OUT1, G_OUT1)
            ff(1)


def shape_tables():
    t = np.arange(SEQ)
    row, col = (t // GRID_W).astype(np.float32), (t % GRID_W).astype(np.float32)
    parts = []
    for rot in (64, 32):
        n = rot // 4
        inv = (np.float32(10000.0) ** (-np.arange(n, dtype=np.float32) / np.float32(n))).astype(np.float32)
        ang = np.concatenate([row[:, None] * inv, col[:, None] * inv], axis=-1).astype(np.float32)
        parts += [np.cos(ang), -np.sin(ang), np.sin(ang)]
    return np.concatenate(parts, axis=-1).astype(np.float32)


def spread_bias(rpb):
    q, k = np.arange(P), np.arange(UW)
    r, c = q // CC, q % CC
    i, kc = k // BAND, k % BAND
    out = np.full((CHUNKS, P, 8, UW), -1e30, dtype=rpb.dtype)
    for j in range(CHUNKS):
        qcol = CC * j + c
        kcol = BAND_START[j] + kc
        start = np.clip(qcol - 8, 0, GRID_W - 16)
        seen = (kcol[None, :] >= start[:, None]) & (kcol[None, :] < start[:, None] + 16)
        rows_ = np.broadcast_to(i[None, :] - r[:, None] + 7, seen.shape)
        cols_ = np.clip(kcol[None, :] - qcol[:, None] + 15, 0, 30)
        for hd in range(8):
            out[j, :, hd, :][seen] = rpb[hd][rows_, cols_][seen]
    return out


def kernel(**inputs):
    import concourse.bacc as bacc
    from concourse.bass_utils import run_bass_kernel_spmd as run

    a = {k: np.asarray(v) for k, v in inputs.items()}
    per_partition = lambda v: np.moveaxis(v.reshape(v.shape[:-1] + (-1, P)), -1, 0).reshape(P, -1)
    cc = np.stack([a["c"][0], a["c_ctx"]], axis=-1).reshape(KT, P, 2)
    cols = np.concatenate([
        per_partition(a["norm_g"]), per_partition(a["b_ada"]), np.moveaxis(cc, 1, 0).reshape(P, -1),
        per_partition(a["mla_q_norm"][0]), per_partition(a["mla_kv_norm"][0]),
        per_partition(a["diff_subln"][0])], axis=1)
    rows = np.concatenate([a["diff_lambda"][0].reshape(-1), a["gqa_qk_norm"][0].reshape(-1)])
    consts = np.concatenate([np.eye(P), np.ones((P, P))], axis=1).astype(np.float32)
    arrays = {
        "x": a["x"], "ctx": a["ctx"], "cols": cols, "rows": rows, "consts": consts, "tables": shape_tables(),
        "na_bias": spread_bias(a["na_rpb"][0]), "w_ada": a["w_ada"], "w_ff1": a["w_ff1"], "w_ff2": a["w_ff2"],
        "w_in_even": a["w_in_even"], "w_out_even": a["w_out_even"], "w_uq": a["mla_w_uq"],
        "w_ukv": a["mla_w_ukv"], "w_in_odd": a["w_in_odd"], "w_out_odd": a["w_out_odd"]}
    nc = bacc.Bacc("TRN2", target_bir_lowering=False, num_devices=1, dynamic_dma_scratch_size=1024)
    feeds, args = {}, []
    for name, v in arrays.items():
        v = np.ascontiguousarray(v)
        feeds[f"in_{name}"] = v
        args.append(nc.dram_tensor(f"in_{name}", v.shape, mybir.dt.from_np(v.dtype), kind="ExternalInput").ap())
    args.append(nc.dram_tensor("out_h", (1, SEQ, D), F32, kind="ExternalOutput").ap())
    build(nc, *args)
    return run(nc, [feeds], core_ids=[0]).results[0]["out_h"]
```
